# Optimizing a Trainium2 kernel written in Bass

```python
import jax, jax.numpy as jnp
from jax import lax
import numpy as np

D_MODEL = 1024
BATCH = 1
SEQ = 128
DEPTH = 1
DEC_BATCH = 1
DEC_SEQ = 1024
PAST_LEN = 128

GRID_W = 64
MIX_WIDTH = D_MODEL
MLSTM_WIDTH = MIX_WIDTH // 2
FOURIER_WIDTH = MIX_WIDTH - MLSTM_WIDTH
MLSTM_HEADS = 4
HEAD_DIM = MLSTM_WIDTH // MLSTM_HEADS
FOURIER_GROUPS = 4
FOURIER_GROUP_DIM = FOURIER_WIDTH // FOURIER_GROUPS
CHUNK = 128
N_GATES = 4 * MLSTM_HEADS
OFF_Q = 0
OFF_K = MLSTM_WIDTH
OFF_V = 2 * MLSTM_WIDTH
OFF_O = 3 * MLSTM_WIDTH
OFF_G = 4 * MLSTM_WIDTH
OFF_F = OFF_G + N_GATES
IN_COLS = OFF_F + FOURIER_WIDTH
N_EXPERTS = 16
CAPACITY_FACTOR = 2
D_EXPERT = 2 * D_MODEL
N_MOD = 6
EPS = 1e-6

kernel_name = "hymba_mlstm_fnet_ec_moe_diffusion_step"

def rmsnorm(x, g):
    xf = x.astype(jnp.float32)
    y = xf * lax.rsqrt(jnp.mean(xf * xf, axis=-1, keepdims=True) + EPS)
    return (y * g).astype(x.dtype)

def mlstm_chunkwise(q, k, v, i_pre, f_pre, C0, n0, m0):
    B, H, T, dh = q.shape
    L = min(CHUNK, T)
    N = T // L
    q = q.reshape(B, H, N, L, dh)
    k = k.reshape(B, H, N, L, dh)
    v = v.reshape(B, H, N, L, dh)
    ig = i_pre.reshape(B, H, N, L)
    b = jnp.cumsum(jax.nn.log_sigmoid(f_pre).reshape(B, H, N, L), axis=-1)
    g = b[..., -1]
    w_log = g[..., None] - b + ig
    m_loc = jnp.max(w_log, axis=-1)
    w = jnp.exp(w_log - m_loc[..., None])
    C_loc = jnp.einsum("bhnl,bhnlv,bhnlk->bhnvk", w, v, k)
    n_loc = jnp.einsum("bhnl,bhnlk->bhnk", w, k)

    def step(carry, inp):
        C, n, m = carry
        g_c, m_l, C_l, n_l = inp
        m_new = jnp.maximum(g_c + m, m_l)
        a = jnp.exp(g_c + m - m_new)
        bb = jnp.exp(m_l - m_new)
        C_new = a[..., None, None] * C + bb[..., None, None] * C_l
        n_new = a[..., None] * n + bb[..., None] * n_l
        return (C_new, n_new, m_new), (C, n, m)

    xs = (jnp.moveaxis(g, 2, 0), jnp.moveaxis(m_loc, 2, 0),
          jnp.moveaxis(C_loc, 2, 0), jnp.moveaxis(n_loc, 2, 0))
    (Cf, nf, mf), (Cs, ns, ms) = lax.scan(step, (C0, n0, m0), xs)
    Cs = jnp.moveaxis(Cs, 0, 2)
    ns = jnp.moveaxis(ns, 0, 2)
    ms = jnp.moveaxis(ms, 0, 2)

    inter_log = b + ms[..., None]
    causal = jnp.tril(jnp.ones((L, L), dtype=bool))
    D = jnp.where(causal, b[..., :, None] - b[..., None, :] + ig[..., None, :], -jnp.inf)
    m_comb = jnp.maximum(inter_log, jnp.max(D, axis=-1))
    S = jnp.einsum("bhnld,bhnsd->bhnls", q, k) * jnp.exp(D - m_comb[..., None])
    w_inter = jnp.exp(inter_log - m_comb)
    num = (jnp.einsum("bhnls,bhnsd->bhnld", S, v)
           + w_inter[..., None] * jnp.einsum("bhnvk,bhnlk->bhnlv", Cs, q))
    den = S.sum(-1) + w_inter * jnp.einsum("bhnk,bhnlk->bhnl", ns, q)
    h = num / jnp.maximum(jnp.abs(den), jnp.exp(-m_comb))[..., None]
    return h.reshape(B, H, T, dh), (Cf, nf, mf)

def mixer(h, w_in, b_in, head_g, w_out, init, grid_w):
    B, T, _ = h.shape
    p = (h @ w_in + b_in).astype(jnp.float32)

    def heads(x):
        return x.reshape(B, T, MLSTM_HEADS, HEAD_DIM).transpose(0, 2, 1, 3)

    q = heads(p[..., OFF_Q:OFF_K])
    k = heads(p[..., OFF_K:OFF_V]) * (HEAD_DIM ** -0.5)
    v = heads(p[..., OFF_V:OFF_O])
    o = p[..., OFF_O:OFF_G]
    gates = p[..., OFF_G:OFF_F].reshape(B, T, 4, MLSTM_HEADS).transpose(2, 0, 3, 1)
    if init is None:
        C0 = jnp.zeros((B, 2, MLSTM_HEADS, HEAD_DIM, HEAD_DIM), jnp.float32)
        n0 = jnp.zeros((B, 2, MLSTM_HEADS, HEAD_DIM), jnp.float32)
        m0 = jnp.zeros((B, 2, MLSTM_HEADS), jnp.float32)
    else:
        C0, n0, m0 = (s.astype(jnp.float32) for s in init)
    h_f, (Cf, nf, mf) = mlstm_chunkwise(q, k, v, gates[0], gates[1], C0[:, 0], n0[:, 0], m0[:, 0])
    h_b, (Cb, nb, mb) = mlstm_chunkwise(jnp.flip(q, 2), jnp.flip(k, 2), jnp.flip(v, 2),
                                        jnp.flip(gates[2], -1), jnp.flip(gates[3], -1),
                                        C0[:, 1], n0[:, 1], m0[:, 1])
    hm = h_f + jnp.flip(h_b, 2)
    hm = hm * lax.rsqrt(jnp.mean(hm * hm, axis=-1, keepdims=True) + EPS) * head_g[:, None, :]
    hm = hm.transpose(0, 2, 1, 3).reshape(B, T, MLSTM_WIDTH) * jax.nn.sigmoid(o)

    u = p[..., OFF_F:]
    if grid_w is None:
        u = u.reshape(B, T, FOURIER_GROUPS, FOURIER_GROUP_DIM)
        fu = jnp.fft.fftn(u, axes=(1, 3), norm="ortho").real
    else:
        rows = T // grid_w
        u = u.reshape(B, rows, grid_w, FOURIER_GROUPS, FOURIER_GROUP_DIM)
        fu = jnp.fft.fftn(u, axes=(1, 2, 4), norm="ortho").real
    fu = fu.reshape(B, T, FOURIER_WIDTH)
    out = jnp.concatenate([hm, fu], axis=-1).astype(h.dtype) @ w_out
    states = (jnp.stack([Cf, Cb], axis=1), jnp.stack([nf, nb], axis=1), jnp.stack([mf, mb], axis=1))
    return out, states

def expert_choice_moe(h, router_w, w1, w3, w2):
    B, T, D = h.shape
    n = B * T
    xf = h.reshape(n, D)
    cap = CAPACITY_FACTOR * n // N_EXPERTS
    aff = jax.nn.softmax((xf @ router_w).astype(jnp.float32), axis=-1)
    gate, idx = lax.top_k(aff.T, cap)
    xe = xf[idx]
    a = jnp.einsum("ecd,edf->ecf", xe, w1)
    bg = jnp.einsum("ecd,edf->ecf", xe, w3)
    ye = jnp.einsum("ecf,efd->ecd", jax.nn.silu(a) * bg, w2) * gate[..., None].astype(h.dtype)
    y = jnp.zeros((n, D), h.dtype).at[idx.reshape(-1)].add(ye.reshape(-1, D))
    return y.reshape(B, T, D)

def modulation(cvec, ada_w, ada_b):
    m = jax.nn.silu(cvec) @ ada_w + ada_b
    return m.reshape(-1, N_MOD, 1, D_MODEL)

def layer(x, mod, init, grid_w, norm1_g, norm2_g, w_in, b_in, head_g, w_out,
          router_w, w1, w3, w2):
    h = rmsnorm(x, norm1_g) * (1 + mod[:, 1]) + mod[:, 0]
    a, states = mixer(h, w_in, b_in, head_g, w_out, init, grid_w)
    x = x + mod[:, 2] * a
    h = rmsnorm(x, norm2_g) * (1 + mod[:, 4]) + mod[:, 3]
    x = x + mod[:, 5] * expert_choice_moe(h, router_w, w1, w3, w2)
    return x, states

def setup_inputs(seed: int = 0) -> dict:
    key = jax.random.key(seed)
    ks = jax.random.split(key, 20)
    D, H, dh, E, F = D_MODEL, MLSTM_HEADS, HEAD_DIM, N_EXPERTS, D_EXPERT
    nrm = jax.random.normal
    b_in = 0.02 * nrm(ks[9], (DEPTH, IN_COLS), jnp.float32)
    fbias = jnp.linspace(3.0, 6.0, H, dtype=jnp.float32)
    b_in = b_in.at[:, OFF_G + H:OFF_G + 2 * H].add(fbias)
    b_in = b_in.at[:, OFF_G + 3 * H:OFF_G + 4 * H].add(fbias)
    return {
        "x_prompt": nrm(ks[0], (BATCH, SEQ, D), jnp.float32),
        "x_sample": nrm(ks[1], (DEC_BATCH, DEC_SEQ, D), jnp.float32),
        "state_C": 0.3 * nrm(ks[2], (DEC_BATCH, DEPTH, 2, H, dh, dh), jnp.float32),
        "state_n": 0.3 * nrm(ks[3], (DEC_BATCH, DEPTH, 2, H, dh), jnp.float32),
        "state_m": nrm(ks[4], (DEC_BATCH, DEPTH, 2, H), jnp.float32),
        "c": nrm(ks[5], (DEC_BATCH, D), jnp.float32),
        "c_ctx": nrm(ks[6], (D,), jnp.float32),
        "ada_w": 0.5 * D ** -0.5 * nrm(ks[7], (DEPTH, D, N_MOD * D), jnp.float32),
        "ada_b": 0.02 * nrm(ks[8], (DEPTH, N_MOD * D), jnp.float32),
        "norm1_g": 1.0 + 0.05 * nrm(ks[10], (DEPTH, D), jnp.float32),
        "norm2_g": 1.0 + 0.05 * nrm(ks[11], (DEPTH, D), jnp.float32),
        "w_in": D ** -0.5 * nrm(ks[12], (DEPTH, D, IN_COLS), jnp.float32),
        "b_in": b_in,
        "head_g": 1.0 + 0.05 * nrm(ks[13], (DEPTH, H, dh), jnp.float32),
        "w_out": MIX_WIDTH ** -0.5 * nrm(ks[14], (DEPTH, MIX_WIDTH, D), jnp.float32),
        "router_w": D ** -0.5 * nrm(ks[15], (DEPTH, D, E), jnp.float32),
        "exp_w1": D ** -0.5 * nrm(ks[16], (DEPTH, E, D, F), jnp.float32),
        "exp_w3": D ** -0.5 * nrm(ks[17], (DEPTH, E, D, F), jnp.float32),
        "exp_w2": F ** -0.5 * nrm(ks[18], (DEPTH, E, F, D), jnp.float32),
        "final_g": 1.0 + 0.05 * nrm(ks[19], (D,), jnp.float32),
    }

def reference(x_prompt, x_sample, state_C, state_n, state_m, c, c_ctx, ada_w, ada_b,
              norm1_g, norm2_g, w_in, b_in, head_g, w_out, router_w, exp_w1, exp_w3,
              exp_w2, final_g):
    xp = x_prompt
    Cs, ns, ms = [], [], []
    for l in range(DEPTH):
        mod_ctx = modulation(c_ctx[None, :], ada_w[l], ada_b[l])
        xp, (Cl, nl, ml) = layer(xp, mod_ctx, None, None, norm1_g[l], norm2_g[l], w_in[l],
                                 b_in[l], head_g[l], w_out[l], router_w[l], exp_w1[l],
                                 exp_w3[l], exp_w2[l])
        Cs.append(Cl)
        ns.append(nl)
        ms.append(ml)
    y_prompt = rmsnorm(xp, final_g)
    new_C = jnp.stack(Cs, axis=1)
    new_n = jnp.stack(ns, axis=1)
    new_m = jnp.stack(ms, axis=1)

    xs = x_sample
    grid_w = GRID_W
    for l in range(DEPTH):
        mod_lat = modulation(c, ada_w[l], ada_b[l])
        init = (state_C[:, l], state_n[:, l], state_m[:, l])
        xs, _ = layer(xs, mod_lat, init, grid_w, norm1_g[l], norm2_g[l], w_in[l], b_in[l],
                      head_g[l], w_out[l], router_w[l], exp_w1[l], exp_w3[l], exp_w2[l])
    y_sample = rmsnorm(xs, final_g)
    return (y_prompt, y_sample, new_C, new_n, new_m)


_drawn_inputs = setup_inputs


def setup_inputs(seed=0):
    import zlib

    import numpy as np

    out = dict(_drawn_inputs(seed))
    spreads = {}
    factors = {'state_C': 4.074, 'state_n': 8.0, 'state_m': 4.565, 'norm2_g': 5.025, 'head_g': 8.0}
    for name, (base, spread) in spreads.items():
        noise = np.random.default_rng([zlib.crc32(name.encode()), seed]).standard_normal(out[name].shape)
        drawn = base * np.exp(spread * noise) if base else spread * noise
        out[name] = __import__('jax').numpy.asarray(drawn.astype(out[name].dtype))
    for name, factor in factors.items():
        out[name] = (out[name] * factor).astype(out[name].dtype)
    return out
```

```python
from contextlib import ExitStack, contextmanager

import concourse.bass as bass
from concourse import mybir
from concourse.alu_op_type import AluOpType as ALU

ACT = mybir.ActivationFunctionType
AX = mybir.AxisListType
F32 = mybir.dt.float32
U32 = mybir.dt.uint32

P = 128
D = 1024
DT = D // P
PROMPT, LATENT = 128, 1024
ROWS = PROMPT + LATENT
TILES = ROWS // P
GRID_W = 64
GRID_H = LATENT // GRID_W
HEADS = 4
WIDTH = 512
HD = WIDTH // HEADS
LANES = 2 * HEADS
N_GATES = 4 * HEADS
OFF_G = 4 * WIDTH
OFF_F = OFF_G + N_GATES
IN_COLS = OFF_F + WIDTH
E = 16
F = 2 * D
FT = F // P
CAP_L = 2 * LATENT // E
CAP_P = 2 * PROMPT // E
N_MOD = 6
MOD_COLS = N_MOD * D
MOD_T = MOD_COLS // P
EPS = 1e-6
K_SCALE = HD ** -0.5
HUGE = 3.0e38
MASKED = 1.0e30
VW = HD + 1


class Shared:
    pass


class Steps:

    def __init__(self, engine, own):
        self.engine, self.own = engine, own
        self.count, self.added, self.latest = {}, {}, None

    def did(self, instruction, sem=None):
        sem = sem or self.own
        instruction.then_inc(sem, 1)
        self.count[sem.name] = self.count.get(sem.name, 0) + 1
        self.added[sem.name] = self.added.get(sem.name, 0) + 1
        self.latest = sem

    def settle(self):
        self.engine.wait_ge(self.latest, self.count[self.latest.name])

    @contextmanager
    def loop(self, engine, times, per):
        with engine.Fori(0, times) as j:
            start = {n: self.count.get(n, 0) for n in per}
            self.count.update({n: j * per[n] + start[n] for n in per})
            self.added = {}
            yield j
            assert self.added == per, self.added
        self.count.update({n: start[n] + times * per[n] for n in per})


def modulation(nc, g):
    NB, RING = MOD_COLS // 512, 3
    ctx = ExitStack()
    with ctx:
        def sb(name, shape):
            return ctx.enter_context(nc.sbuf_tensor(name, shape, F32))

        vec_rows = sb("vec_rows", [32, P])
        bias_rows = sb("bias_rows", [MOD_T, P])
        held = g.y.rearrange("p a b n -> p (a b n)").rearrange("p (s k n) -> p s k n", s=2, k=DT)
        last = sb("ada_slot", [P, DT, 512])
        ada = [held[:, 0], held[:, 1], last[:]]
        mod_row = sb("mod_row", [2, MOD_COLS])
        vecT = sb("vecT", [P, 32])
        biasT = sb("biasT", [P, MOD_T])
        modT = sb("modT", [P, MOD_T, 2])
        gate1_bias = sb("gate1_bias", [P, D])
        ps_row = [ctx.enter_context(nc.psum_tensor(f"ps_row{i}", [P, 512], F32)) for i in range(RING)]
        ps_col = ctx.enter_context(nc.psum_tensor("ps_col", [P, 512], F32))
        ps_gate = [ctx.enter_context(nc.psum_tensor(f"ps_gate{i}", [P, 512], F32)) for i in range(4)]

        small_loaded = g.sem("small_loaded")
        ada_loaded = [g.sem(f"ada_loaded{i}") for i in range(RING)]
        silu_done = g.sem("silu_done")
        vec_turned = g.sem("vec_turned")
        vec_kept = g.sem("vec_kept")
        row_summed = g.sem("row_summed")
        row_kept = g.sem("row_kept")
        mod_turned = g.sem("mod_turned")
        gate_spread = g.sem("gate_spread")
        ada_src = g.ada_w.rearrange("(k p) n -> p k n", p=P)

        with nc.Block() as block:
            @block.sync
            def _(sp):
                sp.dma_start(vec_rows[0:8, :], g.c_ctx).then_inc(small_loaded, 16)
                sp.dma_start(vec_rows[8:16, :], g.c).then_inc(small_loaded, 16)
                sp.dma_start(vec_rows[16:24, :], g.norm1_g).then_inc(small_loaded, 16)
                sp.dma_start(vec_rows[24:32, :], g.norm2_g).then_inc(small_loaded, 16)
                sp.dma_start(bias_rows[:], g.ada_b).then_inc(small_loaded, 16)
                sp.dma_start(g.const[:], g.constants).then_inc(small_loaded, 16)
                sp.dma_start(gate1_bias[:], g.ada_b_row[:, 2 * D:3 * D].to_broadcast([P, D])).then_inc(small_loaded, 16)

                def load(n, s, reused):
                    if reused:
                        sp.wait_ge(row_summed, n - RING + 1)
                    sp.dma_start(ada[s], ada_src[:, :, bass.ts(n, 512)]).then_inc(ada_loaded[s], 16)

                for n in range(RING):
                    load(n, n, False)
                with sp.Fori(1, NB // RING) as j:
                    for s in range(RING):
                        load(j * RING + s, s, True)
                for n in range(4):
                    sp.dma_start(g.w_in_sb[:, 2 * n:2 * n + 2], g.w_in_src[:, 2 * n:2 * n + 2]).then_inc(g.w_in_loaded, 16)
                sp.dma_start(g.b_in_row[:], g.b_in.to_broadcast([P, IN_COLS])).then_inc(g.w_in_loaded, 16)

            @block.scalar
            def _(act):
                act.wait_ge(small_loaded, 16 * 7)
                g.act.did(nc.scalar.activation(vec_rows[0:16, :], vec_rows[0:16, :], ACT.Silu), silu_done)

            @block.tensor
            def _(pe):
                pe.wait_ge(silu_done, 1)
                nc.tensor.transpose(ps_col[:, 0:32], vec_rows[:], g.ident[0:32, 0:32])
                nc.tensor.transpose(ps_col[:, 32:32 + MOD_T], bias_rows[:], g.ident[0:MOD_T, 0:MOD_T]).then_inc(vec_turned, 1)
                pe.wait_ge(vec_kept, 2)

                def block_sum(n, s, half, reused):
                    pe.wait_ge(ada_loaded[s], 16 * (half + 1))
                    if reused:
                        pe.wait_ge(row_kept, n - RING + 1)
                    for k in range(DT):
                        mm = nc.tensor.matmul(ps_row[s][0:2, :], vecT[:, k:16:DT], ada[s][:, k, :],
                                              start=(k == 0), stop=(k == DT - 1))
                    mm.then_inc(row_summed, 1)

                for n in range(RING):
                    block_sum(n, n, 0, False)
                with pe.Fori(1, NB // RING) as j:
                    for s in range(RING):
                        block_sum(j * RING + s, s, j, True)
                pe.wait_ge(row_kept, NB)
                for n in range(4):
                    grp, h = divmod(n, 2)
                    mm = nc.tensor.matmul(ps_gate[n][:], g.pick2[0:2, bass.ts(grp, P)],
                                          mod_row[:, 2 * D + 512 * h:2 * D + 512 * h + 512], start=True, stop=True)
                mm.then_inc(gate_spread, 1)
                for t in range(MOD_T):
                    mm = nc.tensor.transpose(ps_col[:, 2 * t:2 * t + 2], mod_row[:, bass.ts(t, P)], g.ident[0:2, 0:2])
                mm.then_inc(mod_turned, 1)

            @block.vector
            def _(dve):
                dve.wait_ge(vec_turned, 1)
                g.dve.did(nc.vector.tensor_copy(vecT[:], ps_col[:, 0:32]), vec_kept)
                g.dve.did(nc.vector.tensor_copy(biasT[:], ps_col[:, 32:32 + MOD_T]), vec_kept)

                def keep(n, s):
                    dve.wait_ge(row_summed, n + 1)
                    g.dve.did(nc.vector.tensor_copy(mod_row[:, bass.ts(n, 512)], ps_row[s][0:2, :]), row_kept)

                with g.dve.loop(dve, NB // RING, {"row_kept": RING}) as j:
                    for s in range(RING):
                        keep(j * RING + s, s)
                dve.wait_ge(gate_spread, 1)
                for n in range(4):
                    grp, h = divmod(n, 2)
                    g.dve.did(nc.vector.tensor_tensor(g.gate1[:, grp, bass.ts(h, 512)], ps_gate[n][:],
                                                      gate1_bias[:, bass.ts(h, 512)], ALU.add))
                dve.wait_ge(mod_turned, 1)
                g.dve.did(nc.vector.tensor_tensor(modT[:], ps_col[:, 0:2 * MOD_T].rearrange("p (t c) -> p t c", c=2),
                                                  biasT[:, :, None].to_broadcast([P, MOD_T, 2]), ALU.add))
                g.dve.settle()
                for grp in range(2):
                    for scale, shift, gain, off in ((1, 0, 16, 0), (4, 3, 24, 2)):
                        g.dve.did(nc.vector.scalar_tensor_tensor(
                            g.mod[:, grp, off], modT[:, scale * DT:(scale + 1) * DT, grp], 1.0, vecT[:, gain:gain + DT],
                            ALU.add, ALU.mult))
                        g.dve.did(nc.vector.tensor_copy(g.mod[:, grp, off + 1], modT[:, shift * DT:(shift + 1) * DT, grp]))
                    g.dve.did(nc.vector.tensor_copy(g.mod[:, grp, 4], modT[:, 5 * DT:6 * DT, grp]))
                g.dve.settle()


def tile_loop(engine, steps, body, per=None):
    body(0, 0, 0)
    body(1, 1, 0)
    if steps is None:
        with engine.Fori(1, TILES // 2) as j:
            body(j * 2, 0, j)
            body(j * 2 + 1, 1, j)
    else:
        with steps.loop(engine, TILES // 2 - 1, per) as j:
            body(j * 2 + 2, 0, j + 1)
            body(j * 2 + 3, 1, j + 1)
    body(TILES - 1, 0, TILES // 2)


def first(i):
    return isinstance(i, int) and i < 2


def projection(nc, g):
    ctx = ExitStack()
    with ctx:
        def sb(name, shape):
            return ctx.enter_context(nc.sbuf_tensor(name, shape, F32))

        xt = sb("xt", [P, 2, D])
        xn = sb("xn", [P, D])
        squares = ctx.enter_context(nc.sbuf_tensor("squares", [P, D], mybir.dt.bfloat16))
        ms = sb("ms", [P, 2, 4])
        hT = sb("hT", [P, 2, DT, P])
        pr = sb("pr", [P, 2, 5, 512])
        qkT = sb("qkT", [P, 2 * HEADS, P])
        w_gate = g.w_gate
        b_gate = sb("b_gate", [P, 1])

        def bank(name):
            return ctx.enter_context(nc.psum_tensor(name, [P, 512], F32))

        ps_x = [bank(f"ps_x{i}") for i in range(2)]
        ps_p = [bank(f"ps_p{i}") for i in range(2)]
        ps_qk = [bank(f"ps_qk{i}") for i in range(2)]
        ps_g = bank("ps_g")
        ps_y = bank("ps_y")
        sem = g.sem
        x_loaded = [sem(f"x_loaded{i}") for i in range(2)]
        bg_loaded = sem("bg_loaded")
        weights_set = sem("weights_set")
        squares_summed = sem("squares_summed")
        rms_inverted = sem("rms_inverted")
        x_normed = sem("x_normed")
        x_turned = sem("x_turned")
        hT_ready_dve, hT_ready_act = sem("hT_ready_dve"), sem("hT_ready_act")
        block_summed = sem("block_summed")
        block_kept = sem("block_kept")
        qk_turned = sem("qk_turned")
        qk_kept = sem("qk_kept")
        gates_summed = sem("gates_summed")
        gates_kept = sem("gates_kept")
        y_summed = sem("y_summed")
        y_kept = sem("y_kept")
        kvo_stored = [sem(f"kvo_stored{i}") for i in range(2)]
        qk_stored = sem("qk_stored")
        COLS = (0, WIDTH, 2 * WIDTH, 3 * WIDTH, OFF_F)

        with nc.Block() as block:
            @block.sync
            def _(sp):
                with_bias = nc.allow_non_contiguous_dma("sixteen gate biases, one per partition")
                with with_bias:
                    for j, c in enumerate((0, 2, 1, 3)):
                        sp.dma_start(b_gate[32 * j:32 * j + HEADS, :],
                                     g.b_in_col[OFF_G + HEADS * c:OFF_G + HEADS * (c + 1), :]).then_inc(bg_loaded, 16)

                def load(i, par):
                    sp.dma_start(xt[:, par], g.x_rows(i)).then_inc(x_loaded[par], 16)

                def store(i, par):
                    sp.wait_ge(block_kept, 5 * i + 4)
                    sp.dma_start(g.kvo[bass.ts(i, P), :], pr[:, par, 1:4].rearrange("p b n -> p (b n)")).then_inc(kvo_stored[par], 16)
                    sp.wait_ge(qk_kept, 2 * i + 2)
                    sp.dma_start(g.qkT[bass.ts(i, P), :], qkT[:].rearrange("p h n -> p (h n)")).then_inc(qk_stored, 16)

                load(0, 0)
                load(1, 1)

                def body(i, par, half):
                    store(i, par)
                    if not (isinstance(i, int) and i + 2 >= TILES):
                        sp.wait_ge(x_normed, i + 1)
                        load(i + 2, par)

                for i in range(2):
                    body(i, i % 2, 0)
                with sp.Fori(1, 3) as j:
                    for par in range(2):
                        body(j * 2 + par, par, j)
                for i in range(6, TILES):
                    body(i, i % 2, 0)
                sp.wait_ge(kvo_stored[0], 16 * 5)
                sp.wait_ge(kvo_stored[1], 16 * 4)
                sp.wait_ge(qk_stored, 16 * TILES)

            @block.gpsimd
            def _(pool):
                pool.wait_ge(weights_set, 2)

                def body(i, par, half):
                    pool.wait_ge(squares_summed, 2 * i + 2)
                    nc.gpsimd.tensor_tensor(ms[:, par, 2:3], ms[:, par, 1:2], g.minus_half[:, 0:1], ALU.pow).then_inc(rms_inverted, 1)

                tile_loop(pool, None, body)

            @block.scalar
            def _(act):
                def mean_square(i, par, half):
                    act.wait_ge(x_loaded[par], 16 * (half + 1))
                    if not first(i):
                        act.wait_ge(rms_inverted, i - 1)
                    g.act.settle()
                    g.act.did(nc.scalar.activation(squares[:], xt[:, par], ACT.Square, accum_out=ms[:, par, 0:1]), squares_summed)
                    g.act.settle()
                    g.act.did(nc.scalar.activation(ms[:, par, 1:2], ms[:, par, 0:1], ACT.Copy, bias=EPS, scale=1.0 / D), squares_summed)

                mean_square(0, 0, 0)

                def body(i, par, half):
                    grp = 0 if isinstance(i, int) and i == 0 else 1
                    act.wait_ge(x_turned, 2 * i + 2)
                    if not first(i):
                        act.wait_ge(y_summed, 2 * i - 2)
                    for k in range(4, DT):
                        g.act.did(nc.scalar.activation(hT[:, par, k], ps_x[1][:, bass.ts(k - 4, P)], ACT.Identity,
                                                       scale=g.mod[:, grp, 0, k:k + 1], bias=g.mod[:, grp, 1, k:k + 1]), hT_ready_act)
                    if not (isinstance(i, int) and i == TILES - 1):
                        mean_square(i + 1, 1 - par, half + par)
                    if not (isinstance(i, int) and i == 0):
                        act.wait_ge(qk_stored, 16 * i)
                    for j in range(2):
                        act.wait_ge(qk_turned, 2 * i + j + 1)
                        g.act.did(nc.scalar.activation(qkT[:, 4 * j:4 * j + 4], ps_qk[j][:].rearrange("p (h n) -> p h n", n=P),
                                                       ACT.Copy, scale=(1.0, K_SCALE)[j]), qk_kept)
                    for j in range(2):
                        act.wait_ge(y_summed, 2 * i + j + 1)
                        if grp == 0:
                            src = ps_y[:].rearrange("p (a c n) -> p a c n", a=2, n=P)
                            g.act.did(nc.scalar.activation(g.y_prompt[:, 2 * j:2 * j + 2], src, ACT.Copy), y_kept)
                            continue
                        for row in range(2):
                            src = ps_y[:].rearrange("p (ac r b c) -> p ac r b c", ac=4, r=2, b=8)[:, :, row]
                            dst = g.y[:, 2 * j:2 * j + 2].rearrange("p a c (b n) -> p (a c) b n", b=8)
                            dst = dst[:, :, :, bass.ds(i * 16 + (8 * row - 16), 8)]
                            g.act.did(nc.scalar.activation(dst, src, ACT.Copy), y_kept if row else None)

                tile_loop(act, g.act, body, {"squares_summed": 4, "hT_ready_act": 8, "qk_kept": 4, "y_kept": 4, "act_steps": 4})

            @block.tensor
            def _(pe):
                def turn_x(i):
                    pe.wait_ge(x_normed, i + 1)
                    if not (isinstance(i, int) and i == 0):
                        pe.wait_ge(hT_ready_dve, 4 * i)
                        pe.wait_ge(hT_ready_act, 4 * i)
                    for h in range(2):
                        for k in range(4):
                            mm = nc.tensor.transpose(ps_x[h][:, bass.ts(k, P)], xn[:, bass.ts(4 * h + k, P)], g.ident)
                        mm.then_inc(x_turned, 1)

                turn_x(0)
                pe.wait_ge(g.w_in_loaded, 16 * 5)
                pe.wait_ge(weights_set, 2)

                def body(i, par, half):
                    pe.wait_ge(hT_ready_dve, 4 * i + 4)
                    pe.wait_ge(hT_ready_act, 4 * i + 4)

                    def block_sum(b):
                        if b < 2 and isinstance(i, int) and i == 0:
                            pass
                        else:
                            pe.wait_ge(block_kept, 5 * i + b - 1)
                        for k in range(DT):
                            mm = nc.tensor.matmul(ps_p[(par + b) % 2][:], hT[:, par, k], g.w_in_sb[:, k, COLS[b]:COLS[b] + 512],
                                                  start=(k == 0), stop=(k == DT - 1))
                        mm.then_inc(block_summed, 1)

                    def turn(j):
                        pe.wait_ge(block_kept, 5 * i + j + 1)
                        if not (isinstance(i, int) and i == 0):
                            pe.wait_ge(qk_kept, 2 * i + j - 1)
                        for h in range(HEADS):
                            mm = nc.tensor.transpose(ps_qk[j][:, bass.ts(h, P)], pr[:, par, j, bass.ts(h, P)], g.ident)
                        mm.then_inc(qk_turned, 1)

                    block_sum(0)
                    block_sum(1)
                    turn(0)
                    block_sum(2)
                    turn(1)
                    block_sum(3)
                    block_sum(4)
                    if not (isinstance(i, int) and i == 0):
                        pe.wait_ge(gates_kept, i)
                    for k in range(DT):
                        mm = nc.tensor.matmul(ps_g[:, 0:P], w_gate[:, k], hT[:, par, k], start=(k == 0), stop=(k == DT - 1))
                    mm.then_inc(gates_summed, 1)
                    if not (isinstance(i, int) and i == TILES - 1):
                        turn_x(i + 1)
                    basis = g.dft_prompt if isinstance(i, int) and i == 0 else g.dft_cols
                    pe.wait_ge(block_kept, 5 * i + 5)
                    for j in range(2):
                        if j == 0 and isinstance(i, int) and i == 0:
                            pass
                        else:
                            pe.wait_ge(y_kept, 2 * i + j)
                        for a in range(2):
                            mm = nc.tensor.matmul(ps_y[:, 256 * a:256 * a + 256], pr[:, par, 4, bass.ts(2 * j + a, P)], basis,
                                                  start=True, stop=True)
                        mm.then_inc(y_summed, 1)

                tile_loop(pe, None, body)

            @block.vector
            def _(dve):
                g.dve.did(nc.vector.memset(g.minus_half[:], -0.5), weights_set)
                g.dve.did(nc.vector.memset(w_gate[:], 0.0))
                dve.wait_ge(g.w_in_loaded, 16 * 5)
                g.dve.settle()
                for j, c in enumerate((0, 2, 1, 3)):
                    ins = nc.vector.tensor_copy(w_gate[:, :, 32 * j:32 * j + HEADS],
                                                g.w_in_sb[:, :, OFF_G + HEADS * c:OFF_G + HEADS * (c + 1)])
                    g.dve.did(ins, weights_set if j == 3 else None)
                dve.wait_ge(bg_loaded, 16 * 4)

                def normed(i, par, half):
                    dve.wait_ge(rms_inverted, i + 1)
                    dve.wait_ge(x_loaded[par], 16 * (half + 1))
                    if not (isinstance(i, int) and i == 0):
                        dve.wait_ge(x_turned, 2 * i)
                    g.dve.did(nc.vector.tensor_scalar(xn[:], xt[:, par], ms[:, par, 2:3], None, ALU.mult), x_normed)

                def after_norm(i, par, half):
                    grp = 0 if isinstance(i, int) and i == 0 else 1
                    dve.wait_ge(x_turned, 2 * i + 1)
                    if not first(i):
                        dve.wait_ge(y_summed, 2 * i - 2)
                    for k in range(4):
                        g.dve.did(nc.vector.tensor_scalar(hT[:, par, k], ps_x[0][:, bass.ts(k, P)], g.mod[:, grp, 0, k:k + 1],
                                                          g.mod[:, grp, 1, k:k + 1], ALU.mult, ALU.add), hT_ready_dve)
                    for b in range(5):
                        dve.wait_ge(block_summed, 5 * i + b + 1)
                        if b == 0 and not first(i):
                            dve.wait_ge(qk_turned, 2 * i - 2)
                            dve.wait_ge(kvo_stored[par], 16 * half)
                        g.dve.did(nc.vector.tensor_tensor(pr[:, par, b], ps_p[(par + b) % 2][:], g.b_in_row[:, COLS[b]:COLS[b] + 512],
                                                          ALU.add), block_kept)
                        if b == 3 and not (isinstance(i, int) and i == TILES - 1):
                            normed(i + 1, 1 - par, half + par)
                    dve.wait_ge(gates_summed, i + 1)
                    g.dve.did(nc.vector.tensor_copy(g.gate_rows[:, bass.ts(i, P)], ps_g[:, 0:P]), gates_kept)

                normed(0, 0, 0)
                tile_loop(dve, g.dve, after_norm, {"hT_ready_dve": 8, "block_kept": 10, "x_normed": 2, "gates_kept": 2})
                g.dve.settle()
                for j in range(4):
                    s = slice(32 * j, 32 * j + HEADS)
                    g.dve.did(nc.vector.tensor_scalar(g.gate_rows[s, :], g.gate_rows[s, :], b_gate[s, :], None, ALU.add))
                g.dve.settle()


def recurrence(nc, g):
    NR = 32 + HEADS
    ctx = ExitStack()
    with ctx:
        def sb(name, shape):
            return ctx.enter_context(nc.sbuf_tensor(name, shape, F32))

        f_row = sb("f_row", [64, ROWS])
        b_row = sb("b_row", [64, ROWS])
        e_row = sb("e_row", [64, ROWS])
        t_row = sb("t_row", [64, ROWS])
        keep = sb("keep", [64, ROWS])
        wi_row = sb("wi_row", [64, ROWS])
        em_row = sb("em_row", [64, ROWS])
        b_last, e_last, m_last, wi_last = (sb(n, [64, TILES]) for n in ("b_last", "e_last", "m_last", "wi_last"))
        m_new, m_prev = sb("m_new", [64, TILES]), sb("m_prev", [64, TILES])
        m_init = sb("m_init", [64, 1])
        carry = sb("carry", [P, LANES, TILES])
        z_sb = sb("z_sb", [P, 2, 256])
        c_init = sb("c_init", [P, LANES, HD])
        n_init = sb("n_init", [LANES, HD])
        kv = sb("kv", [P, 2, 2, 2 * WIDTH])
        wv = sb("wv", [P, 2, LANES, VW])
        c_end = sb("c_end", [P, LANES, VW])
        c_out = sb("c_out", [P, LANES, HD])
        n_out = sb("n_out", [LANES, HD])
        bk = [ctx.enter_context(nc.psum_tensor(f"bk{i}", [P, 512], F32)) for i in range(8)]
        sem = g.sem
        init_loaded, m_init_loaded = sem("init_loaded"), sem("m_init_loaded")
        m_init_zeroed = sem("m_init_zeroed")
        kv_loaded = [[sem(f"kv_loaded{p}{d}") for d in range(2)] for p in range(2)]
        f_abs_ready, soft_ready = sem("f_abs_ready"), sem("soft_ready")
        exponents_ready, weights_ready = sem("exponents_ready"), sem("weights_ready")
        z_summed, z_kept, f_summed, f_kept = sem("z_summed"), sem("z_kept"), sem("f_summed"), sem("f_kept")
        init_turned, init_kept = sem("init_turned"), sem("init_kept")
        cols_turned, cols_kept = sem("cols_turned"), sem("cols_kept")
        wi_last_ready, carry_spread, carry_kept = sem("wi_last_ready"), sem("carry_spread"), sem("carry_kept")
        wv_fwd, wv_bwd = sem("wv_fwd"), sem("wv_bwd")
        kv_summed, state_kept = sem("kv_summed"), sem("state_kept")
        end_turned, end_kept = sem("end_turned"), sem("end_kept")
        m_stored, states_stored = sem("m_stored"), sem("states_stored")
        m_new_ready = sem("m_new_ready")
        FWD, BWD = slice(0, 32), slice(32, 64)

        def chunks(x):
            return x.rearrange("p (n c) -> p n c", c=P)

        def lane_bank(par, r):
            return bk[(1, 5)[par] + r // 3], VW * (r % 3)

        with nc.Block() as block:
            @block.sync
            def _(sp):
                sp.dma_start(c_init[:], g.state_C.rearrange("(r v) k -> v r k", v=HD)).then_inc(init_loaded, 16)
                sp.dma_start(n_init[:], g.state_n).then_inc(init_loaded, 16)
                sp.wait_ge(m_init_zeroed, 1)
                with nc.allow_non_contiguous_dma("one stabiliser per partition"):
                    for d in range(2):
                        sp.dma_start(m_init[32 * d:32 * d + HEADS, :], g.state_m[HEADS * d:HEADS * d + HEADS, :]).then_inc(m_init_loaded, 16)

                def load(n, par, reused):
                    if reused:
                        sp.wait_ge(kv_summed, n - 1)
                    for d in range(2 if n else 1):
                        tile = TILES - n if d else n
                        sp.dma_start(kv[:, par, d], g.kvo[bass.ts(tile, P), 0:2 * WIDTH]).then_inc(kv_loaded[par][d], 16)

                load(0, 0, False)
                load(1, 1, False)
                for n in range(2, TILES - 1):
                    load(n, n % 2, True)
                sp.wait_ge(m_new_ready, 1)
                with nc.allow_non_contiguous_dma("one stabiliser per partition"):
                    for d in range(2):
                        sp.dma_start(g.new_m[HEADS * d:HEADS * d + HEADS, :], m_new[32 * d:32 * d + HEADS, 0:1]).then_inc(m_stored, 16)
                sp.wait_ge(end_kept, 3)
                sp.dma_start(g.new_C.rearrange("(r v) k -> v r k", v=HD), c_out[:]).then_inc(states_stored, 16)
                sp.dma_start(g.new_n, n_out[:]).then_inc(states_stored, 16)
                sp.wait_ge(m_stored, 32)
                sp.wait_ge(states_stored, 32)

            @block.scalar
            def _(act):
                did, settle = g.act.did, g.act.settle
                act.wait_ge(f_abs_ready, 1)
                did(nc.scalar.activation(t_row[:], t_row[:], ACT.Exp, scale=-1.0))
                settle()
                did(nc.scalar.activation(t_row[:], t_row[:], ACT.Ln, bias=1.0), soft_ready)

                def keep_z(n):
                    act.wait_ge(z_summed, n + 1)
                    if n >= 2:
                        act.wait_ge(f_summed, n - 1)
                    did(nc.scalar.activation(z_sb[:, n % 2], bk[n % 2][:, 0:256], ACT.Copy), z_kept)

                def keep_f(n):
                    act.wait_ge(f_summed, n + 1)
                    grp, kcb = divmod(n, 8)
                    dst = g.fuT[:, grp, PROMPT:ROWS].rearrange("p (r c) -> p r c", c=GRID_W)[:, :, 8 * kcb:8 * kcb + 8]
                    did(nc.scalar.activation(dst, bk[2 + n % 2][:, 0:P].rearrange("p (r c) -> p r c", c=8), ACT.Copy,
                                             scale=(LATENT * HD) ** -0.5), f_kept)

                for n in range(33):
                    if n < 32:
                        keep_z(n)
                    if n >= 1:
                        keep_f(n - 1)
                    if n == 12:
                        act.wait_ge(exponents_ready, 3)
                        for row, scale in ((wi_row, -1.0), (em_row, -1.0), (t_row, 1.0)):
                            did(nc.scalar.activation(row[:], row[:], ACT.Exp, scale=scale), weights_ready)
                act.wait_ge(f_summed, 33)
                did(nc.scalar.activation(g.fuT[:, :, 0:P], bk[0][:].rearrange("p (a n) -> p a n", n=P), ACT.Copy,
                                         scale=(PROMPT * HD) ** -0.5), f_kept)
                for d in range(2):
                    act.wait_ge(end_turned, d + 1)
                    did(nc.scalar.activation(c_out[:, HEADS * d:HEADS * d + HEADS], bk[(4, 0)[d]][:].rearrange("p (r k) -> p r k", k=HD), ACT.Copy), end_kept)
                act.wait_ge(end_turned, 3)
                did(nc.scalar.activation(n_out[:], bk[2][0:LANES, 384:512], ACT.Copy), end_kept)
                settle()

            @block.gpsimd
            def _(pool):
                def weigh(n, par):
                    tile = TILES - n if n else 0
                    d = 1 if n else 0
                    pool.wait_ge(kv_loaded[par][d], 16 * ((n + 1) // 2 if n else 1))
                    if n >= 2:
                        pool.wait_ge(kv_summed, n - 1)
                    nc.gpsimd.tensor_tensor(wv[:, par, HEADS:LANES, 0:HD], kv[:, par, d, WIDTH:].rearrange("p (h v) -> p h v", v=HD),
                                            g.cols[:, 3, tile, HEADS:LANES, None].to_broadcast([P, HEADS, HD]), ALU.mult)
                    nc.gpsimd.tensor_copy(wv[:, par, HEADS:LANES, HD], g.cols[:, 3, tile, HEADS:LANES]).then_inc(wv_bwd, 1)

                pool.wait_ge(cols_kept, 8)
                for n in range(TILES - 1):
                    weigh(n, n % 2)

            @block.tensor
            def _(pe):
                pe.wait_ge(init_loaded, 32)
                for d in range(2):
                    for h in range(HEADS):
                        mm = nc.tensor.transpose(bk[4 + d][:, bass.ts(h, P)], c_init[:, HEADS * d + h], g.ident)
                mm = nc.tensor.transpose(bk[6][:, 0:LANES], n_init[:], g.ident[0:LANES, 0:LANES])
                mm.then_inc(init_turned, 1)

                def z_sum(n):
                    grp, kcb = divmod(n, 8)
                    if n >= 2:
                        pe.wait_ge(z_kept, n - 1)
                    for c, basis in ((0, g.dft_chan_r), (1, g.dft_chan_i)):
                        lhs = g.y[:, grp, c, bass.ts(kcb, P)]
                        mm = nc.tensor.matmul(bk[n % 2][:, 0:256], lhs, basis, start=(c == 0), stop=(c == 1))
                    mm.then_inc(z_summed, 1)

                def f_sum(n):
                    pe.wait_ge(z_kept, n + 1)
                    if n >= 2:
                        pe.wait_ge(f_kept, n - 1)
                    for c, basis in ((0, g.dft_row_c), (1, g.dft_row_s)):
                        mm = nc.tensor.matmul(bk[2 + n % 2][:, 0:P], z_sb[:, n % 2, bass.ts(c, P)], basis, start=(c == 0), stop=(c == 1))
                    mm.then_inc(f_summed, 1)

                for n in range(33):
                    if n < 32:
                        z_sum(n)
                    if n >= 1:
                        f_sum(n - 1)
                pe.wait_ge(z_kept, 32)
                for grp in range(4):
                    for c, basis in ((0, g.dft_chan_r), (1, g.dft_chan_i)):
                        mm = nc.tensor.matmul(bk[0][:, bass.ts(grp, P)], basis[:, 0:P], g.y_prompt[:, grp, c], start=(c == 0), stop=(c == 1))
                mm.then_inc(f_summed, 1)
                pe.wait_ge(weights_ready, 3)
                pe.wait_ge(init_kept, 4)
                for q, row in enumerate((e_row, wi_row, em_row, t_row)):
                    for i in range(TILES):
                        mm = nc.tensor.transpose(bk[4 + q][:, NR * i:NR * i + NR], row[0:NR, bass.ts(i, P)], g.ident[0:NR, 0:NR])
                    mm.then_inc(cols_turned, 1)
                pe.wait_ge(wi_last_ready, 1)
                pe.wait_ge(f_kept, 32)
                for r in range(LANES):
                    mm = nc.tensor.matmul(bk[2][:, TILES * r:TILES * r + TILES], g.pick_lane[0:64, bass.ts(r, P)], wi_last[:], start=True, stop=True)
                mm.then_inc(carry_spread, 1)
                pe.wait_ge(carry_kept, 1)
                pe.wait_ge(cols_kept, 8)
                for n in range(TILES - 1):
                    par = n % 2
                    pe.wait_ge(wv_fwd, n + 1)
                    pe.wait_ge(wv_bwd, n + 1)
                    if n >= 2:
                        pe.wait_ge(state_kept, LANES * (n - 1))
                    for r in range(LANES):
                        bank, at = lane_bank(par, r)
                        d = 1 if n and r >= HEADS else 0
                        mm = nc.tensor.matmul(bank[:, at:at + VW], kv[:, par, d, bass.ts(r % HEADS, P)], wv[:, par, r], start=True, stop=True)
                    mm.then_inc(kv_summed, 1)
                pe.wait_ge(f_kept, 33)
                pe.wait_ge(state_kept, LANES * 8)
                for d in range(2):
                    for h in range(HEADS):
                        mm = nc.tensor.transpose(bk[(4, 0)[d]][:, bass.ts(h, P)], c_end[:, HEADS * d + h, 0:HD], g.ident)
                    mm.then_inc(end_turned, 1)
                nc.tensor.transpose(bk[2][0:LANES, 384:512], c_end[:, :, HD], g.ident).then_inc(end_turned, 1)

            @block.vector
            def _(dve):
                did, settle = g.dve.did, g.dve.settle
                TT, TS, STT = nc.vector.tensor_tensor, nc.vector.tensor_scalar, nc.vector.scalar_tensor_tensor
                did(nc.vector.memset(m_init[:], 0.0), m_init_zeroed)
                did(nc.vector.tensor_copy(f_row[:], g.gate_rows[64:128, :]))
                settle()
                did(STT(t_row[:], f_row[:], -1.0, f_row[:], ALU.mult, ALU.max), f_abs_ready)
                did(nc.vector.memset(keep[:], 1.0))
                did(nc.vector.memset(m_prev[:], 0.0))
                did(nc.vector.memset(g.states[:, 0], 0.0))
                did(nc.vector.memset(g.shared_rows[64:P, :], 0.0))
                did(nc.vector.memset(g.eps[:], EPS))
                settle()
                did(nc.vector.memset(chunks(keep[FWD, :])[:, :, 0], 0.0))
                did(nc.vector.memset(chunks(keep[BWD, :])[:, :, P - 1], 0.0))
                dve.wait_ge(init_turned, 1)
                for d, slot in ((0, 1), (1, TILES - 1)):
                    lanes = slice(HEADS * d, HEADS * d + HEADS)
                    did(nc.vector.tensor_copy(g.states[:, slot, lanes, 0:HD], bk[4 + d][:].rearrange("p (r k) -> p r k", k=HD)), init_kept)
                    did(nc.vector.tensor_copy(g.states[:, slot, lanes, HD], bk[6][:, lanes]), init_kept)
                dve.wait_ge(soft_ready, 1)
                did(STT(f_row[:], f_row[:], 0.0, t_row[:], ALU.min, ALU.subtract))
                settle()
                did(nc.vector.tensor_tensor_scan(b_row[FWD, :], keep[FWD, :], f_row[FWD, :], 0.0, ALU.mult, ALU.add))
                did(nc.vector.tensor_tensor_scan(b_row[BWD, ::-1], keep[BWD, ::-1], f_row[BWD, ::-1], 0.0, ALU.mult, ALU.add))
                settle()
                did(TT(e_row[:], g.gate_rows[0:64, :], b_row[:], ALU.subtract))
                did(TS(keep[:], keep[:], -1.0, HUGE, ALU.add, ALU.mult))
                settle()
                did(nc.vector.tensor_tensor_scan(g.m_row[FWD, :], keep[FWD, :], e_row[FWD, :], 0.0, ALU.add, ALU.max))
                did(nc.vector.tensor_tensor_scan(g.m_row[BWD, ::-1], keep[BWD, ::-1], e_row[BWD, ::-1], 0.0, ALU.add, ALU.max))
                settle()
                for rows, at in ((FWD, P - 1), (BWD, 0)):
                    did(nc.vector.tensor_copy(b_last[rows, :], chunks(b_row[rows, :])[:, :, at]))
                    did(nc.vector.tensor_copy(e_last[rows, :], chunks(g.m_row[rows, :])[:, :, at]))
                dve.wait_ge(m_init_loaded, 32)
                settle()
                did(TS(m_new[:, 0:1], e_last[:, 0:1], 0.0, b_last[:, 0:1], ALU.max, ALU.add), m_new_ready)
                did(nc.vector.tensor_tensor_scan(m_new[FWD, 1:], e_last[FWD, 1:], b_last[FWD, 1:], m_init[FWD, :], ALU.max, ALU.add))
                did(nc.vector.tensor_tensor_scan(m_new[BWD, 1:][:, ::-1], e_last[BWD, 1:][:, ::-1], b_last[BWD, 1:][:, ::-1],
                                                 m_init[BWD, :], ALU.max, ALU.add))
                did(nc.vector.tensor_copy(m_prev[FWD, 1:2], m_init[FWD, :]))
                did(nc.vector.tensor_copy(m_prev[BWD, TILES - 1:TILES], m_init[BWD, :]))
                settle()
                did(nc.vector.tensor_copy(m_prev[FWD, 2:], m_new[FWD, 1:TILES - 1]))
                did(nc.vector.tensor_copy(m_prev[BWD, 1:TILES - 1], m_new[BWD, 2:]))
                settle()
                spread = [64, TILES, P]
                did(TT(chunks(g.m_row), chunks(g.m_row), m_prev[:, :, None].to_broadcast(spread), ALU.max))
                settle()
                did(TT(chunks(wi_row[:]), chunks(g.m_row), m_prev[:, :, None].to_broadcast(spread), ALU.subtract), exponents_ready)
                did(TT(em_row[:], b_row[:], g.m_row[:], ALU.add), exponents_ready)
                for rows, at in ((FWD, P - 1), (BWD, 0)):
                    did(nc.vector.tensor_copy(m_last[rows, :], chunks(g.m_row[rows, :])[:, :, at]))
                settle()
                did(TT(chunks(t_row[:]), chunks(e_row[:]), m_last[:, :, None].to_broadcast(spread), ALU.subtract), exponents_ready)
                dve.wait_ge(weights_ready, 1)
                for rows, at in ((FWD, P - 1), (BWD, 0)):
                    did(nc.vector.tensor_copy(wi_last[rows, :], chunks(wi_row[rows, :])[:, :, at]), wi_last_ready if at == 0 else None)
                for q in range(4):
                    dve.wait_ge(cols_turned, q + 1)
                    src = bk[4 + q][:, 0:NR * TILES].rearrange("p (n c) -> p n c", c=NR)
                    for d in range(2):
                        did(TS(g.cols[:, q, :, HEADS * d:HEADS * d + HEADS], src[:, :, 32 * d:32 * d + HEADS],
                               K_SCALE if q == 3 else 1.0, None, ALU.mult), cols_kept)
                dve.wait_ge(carry_spread, 1)
                did(nc.vector.tensor_copy(carry[:], bk[2][:, 0:LANES * TILES].rearrange("p (r n) -> p r n", n=TILES)), carry_kept)
                settle()

                def weigh(n, par):
                    dve.wait_ge(kv_loaded[par][0], 16 * (n // 2 + 1))
                    if n >= 2:
                        dve.wait_ge(kv_summed, n - 1)
                    did(TT(wv[:, par, 0:HEADS, 0:HD], kv[:, par, 0, WIDTH:].rearrange("p (h v) -> p h v", v=HD),
                           g.cols[:, 3, n, 0:HEADS, None].to_broadcast([P, HEADS, HD]), ALU.mult))
                    did(nc.vector.tensor_copy(wv[:, par, 0:HEADS, HD], g.cols[:, 3, n, 0:HEADS]), wv_fwd)

                weigh(0, 0)
                for n in range(TILES - 1):
                    par = n % 2
                    if n + 1 < TILES - 1:
                        weigh(n + 1, 1 - par)
                    dve.wait_ge(kv_summed, n + 1)
                    if n:
                        settle()
                    for r in range(LANES):
                        bank, at = lane_bank(par, r)
                        src = bank[:, at:at + VW]
                        if n == 0:
                            did(nc.vector.tensor_copy(c_end[:, r], src), state_kept)
                        else:
                            frm, to = (n, n + 1) if r < HEADS else (TILES - n, TILES - 1 - n)
                            did(STT(g.states[:, to, r], g.states[:, frm, r], carry[:, r, frm:frm + 1], src, ALU.mult, ALU.add), state_kept)
                settle()


def below(i, n):
    return isinstance(i, int) and i < n


def mixing(nc, g):
    ctx = ExitStack()
    with ctx:
        def sb(name, shape):
            return ctx.enter_context(nc.sbuf_tensor(name, shape, F32))

        va = sb("va", [P, 2, HEADS, VW])
        o_in = sb("o_in", [P, 2, WIDTH])
        qk = sb("qk", [P, 2, 2 * HEADS, P])
        x_in = sb("x_in", [P, 2, D])
        wgt = sb("wgt", [P, 2, HEADS, P])
        num = sb("num", [P, 2, HEADS, VW])
        den = sb("den", [P, LANES])
        hm, hm2 = sb("hm", [P, HEADS, HD]), sb("hm2", [P, HEADS, HD])
        hms = sb("hms", [P, HEADS])
        og, gain = sb("og", [P, WIDTH]), sb("gain", [P, WIDTH])
        head_g = sb("head_g_row", [P, WIDTH])
        mixT = sb("mixT", [P, 2, DT, P])
        x2 = sb("x2", [P, 2, D])
        xn2 = sb("xn2", [P, D])
        squares = ctx.enter_context(nc.sbuf_tensor("squares2", [P, 512], mybir.dt.bfloat16))
        ss = sb("ss", [P, 4])
        h2T = sb("h2T", [P, DT, P])
        router = sb("router", [P, DT, E])
        logits = sb("logits", [P, P])
        aff = sb("aff", [P, E])
        soft = sb("soft", [P, 4])

        def bank(name):
            return ctx.enter_context(nc.psum_tensor(name, [P, 512], F32))

        b_s, b_m = bank("b_s"), bank("b_m")
        b_n = [bank(f"b_n{i}") for i in range(2)]
        b_i = [bank(f"b_i{i}") for i in range(2)]
        b_z = [bank(f"b_z{i}") for i in range(2)]
        ps_logits, ps_affT = b_z[1][0:E, 0:P], b_z[1][0:E, 0:P]
        sem = g.sem
        pair = lambda name: [sem(f"{name}{i}") for i in range(2)]
        qk_loaded, v_loaded, o_loaded, xr_loaded = pair("qk_loaded"), pair("v_loaded"), pair("o_loaded"), pair("xr_loaded")
        stream_stored = pair("stream_stored")
        normed_stored, consts_loaded, ones_set = sem("normed_stored"), sem("consts_loaded"), sem("ones_set")
        (scores_summed, m_spread, x_ready, w_ready, p_ready, inter_summed, inter_kept, intra_summed, comb_done,
         out_summed, out_kept, x2_ready, sq_summed, rms2_ready, xn2_ready, x2_turned, h2T_dve, h2T_act,
         logits_summed, logits_kept, logits_turned, negmax_ready, soft_exped, aff_ready, aff_turned, aff_kept,
         hm_ready, hm_turned, mix_act, mix_pool, og_exped, og_ready, gain_ready, hms_ready, rh_ready, ss_steps) = (
            sem(n) for n in (
                "scores_summed", "m_spread", "x_ready", "w_ready", "p_ready", "inter_summed", "inter_kept", "intra_summed",
                "comb_done", "out_summed", "out_kept", "x2_ready", "sq_summed", "rms2_ready", "xn2_ready", "x2_turned",
                "h2T_dve", "h2T_act", "logits_summed", "logits_kept", "logits_turned", "negmax_ready", "soft_exped",
                "aff_ready", "aff_turned", "aff_kept", "hm_ready", "hm_turned", "mix_act", "mix_pool", "og_exped",
                "og_ready", "gain_ready", "hms_ready", "rh_ready", "ss_steps"))

        def group(t):
            return 0 if below(t, 1) else 1

        def turns(engine, steps, turn, per=None):
            tile_loop(engine, steps, turn, per)
            turn(TILES, TILES % 2, TILES // 2)
            turn(TILES + 1, (TILES + 1) % 2, (TILES + 1) // 2)

        with nc.Block() as block:
            @block.sync
            def _(sp):
                sp.dma_start(head_g[:], g.head_g.to_broadcast([P, WIDTH])).then_inc(consts_loaded, 16)
                sp.dma_start(router[:], g.router_w.rearrange("(k p) e -> p k e", p=P)).then_inc(consts_loaded, 16)

                def load(i, par, fresh):
                    if not fresh:
                        sp.wait_ge(inter_summed, 2 * i - 2)
                        sp.wait_ge(intra_summed, 2 * i - 2)
                        sp.wait_ge(og_exped, i - 1)
                    sp.dma_start(qk[:, par].rearrange("p h n -> p (h n)"), g.qkT[bass.ts(i, P), :]).then_inc(qk_loaded[par], 16)
                    sp.dma_start(va[:, par, :, 0:HD], g.kvo[bass.ts(i, P), WIDTH:2 * WIDTH].rearrange("p (h v) -> p h v", v=HD)).then_inc(v_loaded[par], 16)
                    sp.dma_start(o_in[:, par], g.kvo[bass.ts(i, P), 2 * WIDTH:3 * WIDTH]).then_inc(o_loaded[par], 16)

                def load_x(i, par):
                    sp.dma_start(x_in[:, par], g.x_rows(i)).then_inc(xr_loaded[par], 16)

                load(0, 0, True)
                load_x(0, 0)
                for n in range(DT // 2):
                    sp.dma_start(g.w_out_sb[:, 2 * n:2 * n + 2], g.w_out_src[:, 2 * n:2 * n + 2]).then_inc(g.w_out_loaded, 16)
                load_x(1, 1)

                def turn(i, par, half):
                    if not (isinstance(i, int) and i >= TILES - 1):
                        load(i + 1, 1 - par, below(i, 1))
                    if below(i, 1) or (isinstance(i, int) and i > TILES):
                        return
                    sp.wait_ge(x2_ready, 2 * i)
                    sp.dma_start(g.stream[bass.ts(i - 1, P), :], x2[:, 1 - par]).then_inc(stream_stored[1 - par], 16)
                    if not (isinstance(i, int) and i >= TILES - 1):
                        load_x(i + 1, 1 - par)
                    sp.wait_ge(xn2_ready, i)
                    sp.dma_start(g.normed[bass.ts(i - 1, P), :], xn2[:]).then_inc(normed_stored, 16)

                turns(sp, None, turn)
                for par, n in ((0, 5), (1, 4)):
                    sp.wait_ge(stream_stored[par], 16 * n)
                sp.wait_ge(normed_stored, 16 * TILES)

            @block.gpsimd
            def _(pool):
                pool.wait_ge(consts_loaded, 32)

                def turn(i, par, half):
                    T = i - 1
                    if not (isinstance(i, int) and i >= TILES):
                        if not below(i, 2):
                            pool.wait_ge(out_summed, 2 * i - 2)
                        nc.gpsimd.tensor_copy(mixT[:, par, HEADS:DT], g.fuT[:, :, bass.ts(i, P)]).then_inc(mix_pool, 1)
                        pool.wait_ge(og_ready, i + 1)
                        if not below(i, 1):
                            pool.wait_ge(hm_ready, i)
                        nc.gpsimd.tensor_tensor(gain[:], og[:], head_g[:], ALU.mult).then_inc(gain_ready, 1)
                    if not below(i, 1) and not (isinstance(i, int) and i > TILES):
                        pool.wait_ge(sq_summed, 2 * i)
                        if not below(i, 2):
                            pool.wait_ge(xn2_ready, i - 1)
                        nc.gpsimd.tensor_tensor(ss[:, 2:3], ss[:, 0:1], ss[:, 1:2], ALU.add).then_inc(ss_steps, 1)
                        pool.wait_ge(ss_steps, T * 2 + 1)
                        nc.gpsimd.tensor_tensor(ss[:, 2:3], ss[:, 2:3], g.eps[:], ALU.add).then_inc(ss_steps, 1)
                        pool.wait_ge(ss_steps, T * 2 + 2)
                        nc.gpsimd.tensor_tensor(ss[:, 3:4], ss[:, 2:3], g.minus_half[:, 0:1], ALU.pow).then_inc(rms2_ready, 1)
                    if not (isinstance(i, int) and i >= TILES):
                        pool.wait_ge(hms_ready, i + 1)
                        nc.gpsimd.tensor_tensor(hms[:], hms[:], g.minus_half[:], ALU.pow).then_inc(rh_ready, 1)

                turns(pool, None, turn)

            @block.scalar
            def _(act):
                did = g.act.did

                def front(i, par, half):
                    act.wait_ge(o_loaded[par], 16 * (half + 1))
                    if not below(i, 1):
                        act.wait_ge(gain_ready, i)
                    did(nc.scalar.activation(og[:], o_in[:, par], ACT.Exp, scale=-1.0), og_exped)

                def weigh(i, d):
                    act.wait_ge(x_ready, 2 * i + (d + 1))
                    did(nc.scalar.activation(wgt[:, d], wgt[:, d], ACT.Exp, scale=-1.0), w_ready)

                def inter(i, d):
                    act.wait_ge(inter_summed, 2 * i + (d + 1))
                    if not below(i, 1):
                        act.wait_ge(hm_ready, i)
                    for h in range(HEADS):
                        did(nc.scalar.activation(num[:, d, h], b_i[h // 2][:, VW * (h % 2):VW * (h % 2) + VW], ACT.Copy,
                                                 scale=g.cols[:, 1, i, HEADS * d + h:HEADS * d + h + 1] if isinstance(i, int)
                                                 else g.cols[:, 1, bass.ds(i, 1), HEADS * d + h]), inter_kept if h == HEADS - 1 else None)

                def back(T, i, par):
                    for h in range(2):
                        act.wait_ge(x2_ready, 2 * i + (h - 1))
                        if not below(i, 2):
                            act.wait_ge(rms2_ready, i - 1)
                        g.act.settle()
                        did(nc.scalar.activation(squares[:], x2[:, 1 - par, bass.ts(h, 512)], ACT.Square, scale=D ** -0.5, accum_out=ss[:, h:h + 1]), sq_summed)

                def turn(i, par, half):
                    T = i - 1
                    fr = not (isinstance(i, int) and i >= TILES)
                    bk = not below(i, 1) and not (isinstance(i, int) and i > TILES)
                    if fr:
                        front(i, par, half)
                        weigh(i, 0)
                    if not below(i, 2):
                        act.wait_ge(negmax_ready, i - 1)
                        if not below(i, 3):
                            act.wait_ge(aff_ready, i - 2)
                        did(nc.scalar.activation(aff[:], b_z[1][:, 0:E], ACT.Exp, bias=soft[:, 0:1], accum_out=soft[:, 1:2]), soft_exped)
                    if fr:
                        inter(i, 0)
                        weigh(i, 1)
                    if bk:
                        back(T, i, par)
                    if fr:
                        inter(i, 1)
                    if bk:
                        act.wait_ge(x2_turned, i)
                        for k in range(4, DT):
                            did(nc.scalar.activation(h2T[:, k], b_z[1][:, bass.ts(k - 4, P)], ACT.Identity,
                                                     scale=g.mod[:, group(T), 2, k:k + 1], bias=g.mod[:, group(T), 3, k:k + 1]),
                                h2T_act if k == DT - 1 else None)
                    if fr:
                        act.wait_ge(hm_turned, i + 1)
                        if not below(i, 2):
                            act.wait_ge(out_summed, 2 * i - 2)
                        did(nc.scalar.activation(mixT[:, par, 0:HEADS], b_z[0][:].rearrange("p (h n) -> p h n", n=P), ACT.Copy), mix_act)

                turns(act, g.act, turn, {"og_exped": 2, "w_ready": 4, "inter_kept": 4, "act_steps": 18, "sq_summed": 4,
                                         "soft_exped": 2, "h2T_act": 2, "mix_act": 2})

            @block.tensor
            def _(pe):
                def score(i, par, half):
                    pe.wait_ge(qk_loaded[par], 16 * (half + 1))
                    if not below(i, 1):
                        pe.wait_ge(p_ready, 2 * i)
                    for h in range(HEADS):
                        mm = nc.tensor.matmul(b_s[:, bass.ts(h, P)], qk[:, par, HEADS + h], qk[:, par, h], start=True, stop=True)
                    mm.then_inc(scores_summed, 1)

                def spread(i, d):
                    if not below(2 * i + d, 1):
                        pe.wait_ge(x_ready, 2 * i + d)
                    for h in range(HEADS):
                        mm = nc.tensor.matmul(b_m[:, bass.ts(h, P)], g.pick_lane[:, bass.ts(HEADS * d + h, P)],
                                              g.shared_rows[:, bass.ts(i, P)], start=True, stop=True)
                    mm.then_inc(m_spread, 1)

                def inter(i, par, d):
                    if not below(2 * i + d, 1):
                        pe.wait_ge(inter_kept, 2 * i + d)
                    for h in range(HEADS):
                        mm = nc.tensor.matmul(b_i[h // 2][:, VW * (h % 2):VW * (h % 2) + VW], qk[:, par, h],
                                              g.states[:, i, HEADS * d + h] if isinstance(i, int) else
                                              g.states[:, bass.ds(i, 1), HEADS * d + h].rearrange("p a v -> p (a v)"), start=True, stop=True)
                    mm.then_inc(inter_summed, 1)

                def intra(i, par, half, d):
                    pe.wait_ge(p_ready, 2 * i + (d + 1))
                    pe.wait_ge(v_loaded[par], 16 * (half + 1))
                    if not below(2 * i + d, 1):
                        pe.wait_ge(comb_done, 2 * i + d)
                    for h in range(HEADS):
                        mm = nc.tensor.matmul(b_n[h // 2][:, VW * (h % 2):VW * (h % 2) + VW], wgt[:, d, h], va[:, par, h], start=True, stop=True)
                    mm.then_inc(intra_summed, 1)

                def project(i, par, h):
                    pe.wait_ge(mix_act, i)
                    pe.wait_ge(mix_pool, i)
                    for k in range(DT):
                        mm = nc.tensor.matmul(b_z[h][:], mixT[:, 1 - par, k], g.w_out_sb[:, k, bass.ts(h, 512)], start=(k == 0), stop=(k == DT - 1))
                    mm.then_inc(out_summed, 1)

                def route(i):
                    pe.wait_ge(xn2_ready, i)
                    pe.wait_ge(out_kept, 2 * i)
                    for k in range(DT):
                        mm = nc.tensor.transpose(b_z[k // 4][:, bass.ts(k % 4, P)], xn2[:, bass.ts(k, P)], g.ident)
                    mm.then_inc(x2_turned, 1)
                    pe.wait_ge(h2T_dve, i)
                    pe.wait_ge(h2T_act, i)
                    if not below(i, 2):
                        pe.wait_ge(logits_kept, i - 1)
                    for k in range(DT):
                        mm = nc.tensor.matmul(ps_logits, router[:, k], h2T[:, k], start=(k == 0), stop=(k == DT - 1))
                    mm.then_inc(logits_summed, 1)

                pe.wait_ge(ones_set, 1)

                def turn(i, par, half):
                    fr = not (isinstance(i, int) and i >= TILES)
                    bk = not below(i, 1) and not (isinstance(i, int) and i > TILES)
                    if fr:
                        score(i, par, half)
                        spread(i, 0)
                    if bk:
                        if below(i, 2):
                            pe.wait_ge(g.w_out_loaded, 16 * (DT // 2))
                            pe.wait_ge(consts_loaded, 32)
                        project(i, par, 0)
                    if not below(i, 2):
                        pe.wait_ge(aff_ready, i - 1)
                        nc.tensor.transpose(ps_affT, aff[:], g.ident).then_inc(aff_turned, 1)
                    if fr:
                        inter(i, par, 0)
                        intra(i, par, half, 0)
                        spread(i, 1)
                    if bk:
                        if not below(i, 2):
                            pe.wait_ge(aff_kept, i - 1)
                        project(i, par, 1)
                    if fr:
                        inter(i, par, 1)
                        intra(i, par, half, 1)
                    if bk:
                        route(i)
                    if fr:
                        pe.wait_ge(hm_ready, i + 1)
                        for h in range(HEADS):
                            mm = nc.tensor.transpose(b_z[0][:, bass.ts(h, P)], hm[:, h], g.ident)
                        mm.then_inc(hm_turned, 1)
                    if bk:
                        pe.wait_ge(logits_kept, i)
                        if not below(i, 2):
                            pe.wait_ge(aff_ready, i - 1)
                        nc.tensor.transpose(b_z[1][:, 0:P], logits[:], g.ident).then_inc(logits_turned, 1)

                turns(pe, None, turn)

            @block.vector
            def _(dve):
                did, settle = g.dve.did, g.dve.settle
                TT, TS, STT = nc.vector.tensor_tensor, nc.vector.tensor_scalar, nc.vector.scalar_tensor_tensor
                COPY = nc.vector.tensor_copy
                did(nc.vector.memset(logits[:], 0.0))
                did(nc.vector.memset(va[:, :, :, HD], 1.0), ones_set)
                settle()

                def exponents(i, d):
                    dve.wait_ge(m_spread, 2 * i + (d + 1))
                    if not below(i, 1):
                        dve.wait_ge(intra_summed, 2 * i + (d - 1))
                    for h in range(HEADS):
                        e = g.cols[:, 0, i, HEADS * d + h:HEADS * d + h + 1] if isinstance(i, int) else g.cols[:, 0, bass.ds(i, 1), HEADS * d + h]
                        did(STT(wgt[:, d, h], b_m[:, bass.ts(h, P)], e, g.masks[:, bass.ts(d, P)], ALU.subtract, ALU.max),
                            x_ready if h == HEADS - 1 else None)

                def weighted(i, d):
                    dve.wait_ge(w_ready, 2 * i + (d + 1))
                    dve.wait_ge(scores_summed, i + 1)
                    did(TT(wgt[:, d], wgt[:, d], b_s[:].rearrange("p (h n) -> p h n", n=P), ALU.mult), p_ready)

                def residual(i, par, half, h):
                    grp = group(i - 1)
                    cols = bass.ts(h, 512)
                    dve.wait_ge(out_summed, 2 * i + (h - 1))
                    if h == 0:
                        th = half if par else half - 1
                        dve.wait_ge(xr_loaded[1 - par], 16 * (th + 1))
                        if not below(i, 3):
                            dve.wait_ge(stream_stored[1 - par], 16 * th)
                    did(TT(x2[:, 1 - par, cols], b_z[h][:], g.gate1[:, grp, cols], ALU.mult), out_kept)
                    settle()
                    did(TT(x2[:, 1 - par, cols], x2[:, 1 - par, cols], x_in[:, 1 - par, cols], ALU.add), x2_ready)

                def combine(i, d):
                    dve.wait_ge(inter_kept, 2 * i + (d + 1))
                    dve.wait_ge(intra_summed, 2 * i + (d + 1))
                    for b in range(2):
                        did(TT(num[:, d, 2 * b:2 * b + 2], num[:, d, 2 * b:2 * b + 2], b_n[b][:, 0:2 * VW].rearrange("p (h v) -> p h v", v=VW),
                               ALU.add), comb_done if b else None)

                def outputs(i):
                    settle()
                    nums = num[:].rearrange("p d h v -> p (d h) v")
                    did(STT(den[:], nums[:, :, HD], -1.0, nums[:, :, HD], ALU.mult, ALU.max))
                    settle()
                    em = g.cols[:, 2, i] if isinstance(i, int) else g.cols[:, 2, bass.ds(i, 1)].rearrange("p a r -> p (a r)")
                    did(TT(den[:], den[:], em, ALU.max))
                    settle()
                    did(nc.vector.reciprocal(den[:], den[:]))
                    settle()
                    if not below(i, 1):
                        dve.wait_ge(hm_turned, i)
                    wide = [P, HEADS, HD]
                    did(TT(hm[:], num[:, 0, :, 0:HD], den[:, 0:HEADS, None].to_broadcast(wide), ALU.mult))
                    did(TT(hm2[:], num[:, 1, :, 0:HD], den[:, HEADS:, None].to_broadcast(wide), ALU.mult))
                    settle()
                    did(TT(hm[:], hm[:], hm2[:], ALU.add))
                    settle()
                    did(TT(hm2[:], hm[:], hm[:], ALU.mult))
                    settle()
                    did(nc.vector.tensor_reduce(hms[:], hm2[:], AX.X, ALU.add))
                    settle()
                    did(TS(hms[:], hms[:], 1.0 / HD, EPS, ALU.mult, ALU.add), hms_ready)
                    dve.wait_ge(gain_ready, i + 1)
                    did(TT(hm[:], hm[:], gain[:].rearrange("p (h v) -> p h v", v=HD), ALU.mult))
                    settle()
                    dve.wait_ge(rh_ready, i + 1)
                    did(TT(hm[:], hm[:], hms[:, :, None].to_broadcast(wide), ALU.mult), hm_ready)

                def turn(i, par, half):
                    fr = not (isinstance(i, int) and i >= TILES)
                    bk = not below(i, 1) and not (isinstance(i, int) and i > TILES)
                    if fr:
                        exponents(i, 0)
                        dve.wait_ge(og_exped, i + 1)
                        did(TS(og[:], og[:], 1.0, None, ALU.add))
                        weighted(i, 0)
                        settle()
                        did(nc.vector.reciprocal(og[:], og[:]), og_ready)
                    if not below(i, 2):
                        dve.wait_ge(logits_turned, i - 1)
                        did(nc.vector.tensor_reduce(soft[:, 0:1], b_z[1][:, 0:E], AX.X, ALU.max, negate=True), negmax_ready)
                        dve.wait_ge(soft_exped, i - 1)
                        did(nc.vector.reciprocal(soft[:, 2:3], soft[:, 1:2]))
                        settle()
                        did(TS(aff[:], aff[:], soft[:, 2:3], None, ALU.mult), aff_ready)
                    if bk:
                        residual(i, par, half, 0)
                    if not below(i, 2):
                        dve.wait_ge(aff_turned, i - 1)
                        did(COPY(g.aff_rows[:, bass.ts(i - 2, P)], ps_affT), aff_kept)
                    if fr:
                        combine(i, 0)
                        exponents(i, 1)
                        weighted(i, 1)
                    if bk:
                        residual(i, par, half, 1)
                        dve.wait_ge(rms2_ready, i)
                        if not below(i, 2):
                            dve.wait_ge(x2_turned, i - 1)
                            dve.wait_ge(normed_stored, 16 * i - 16)
                        did(TS(xn2[:], x2[:, 1 - par], ss[:, 3:4], None, ALU.mult), xn2_ready)
                    if fr:
                        combine(i, 1)
                    if bk:
                        dve.wait_ge(x2_turned, i)
                        for k in range(4):
                            did(TS(h2T[:, k], b_z[0][:, bass.ts(k, P)], g.mod[:, group(i - 1), 2, k:k + 1], g.mod[:, group(i - 1), 3, k:k + 1],
                                   ALU.mult, ALU.add), h2T_dve if k == 3 else None)
                    if fr:
                        outputs(i)
                    if bk:
                        dve.wait_ge(logits_summed, i)
                        if not below(i, 2):
                            dve.wait_ge(logits_turned, i - 1)
                        did(COPY(logits[0:E, :], ps_logits), logits_kept)

                turns(dve, g.dve, turn, {
                    "dve_steps": 44, "x_ready": 4, "p_ready": 4, "og_ready": 2, "negmax_ready": 2, "out_kept": 4, "x2_ready": 4,
                    "comb_done": 4, "aff_ready": 2, "xn2_ready": 2, "aff_kept": 2, "h2T_dve": 2, "hms_ready": 2, "hm_ready": 2,
                    "logits_kept": 2})
                settle()


def routing(nc, g):
    ctx = ExitStack()
    with ctx:
        def sb(name, shape, dt=F32):
            return ctx.enter_context(nc.sbuf_tensor(name, shape, dt))

        left = sb("left", [E, LATENT])
        top, top_p = sb("top", [E, CAP_L]), sb("top_p", [E, CAP_P])
        at, at_p = sb("at", [E, CAP_L], U32), sb("at_p", [E, CAP_P], U32)
        at_f, at_pf = sb("at_f", [E, CAP_L]), sb("at_pf", [E, CAP_P])
        ps = [ctx.enter_context(nc.psum_tensor(f"ps_route{i}", [P, 512], F32)) for i in range(4)]
        picked, slots_turned = g.sem("picked"), g.sem("slots_turned")

        with nc.Block() as block:
            @block.sync
            def _(sp):
                for p in range(g.RING // 2):
                    g.load_pair(sp, 0, p)

            @block.tensor
            def _(pe):
                pe.wait_ge(picked, 4)
                ident = g.ident[0:E, 0:E]
                nc.tensor.transpose(ps[0][:, 0:E], top[:], ident)
                nc.tensor.transpose(ps[1][:, 0:E], at_f[:], ident)
                nc.tensor.transpose(ps[2][0:CAP_P, 0:E], top_p[:], ident)
                nc.tensor.transpose(ps[3][0:CAP_P, 0:E], at_pf[:], ident).then_inc(slots_turned, 1)

            @block.vector
            def _(dve):
                did, settle = g.dve.did, g.dve.settle

                def pick(src, values, places, n):
                    for r in range(n // 8):
                        eight = slice(8 * r, 8 * r + 8)
                        did(nc.vector.max(values[:, eight], src))
                        settle()
                        did(nc.vector.max_index(places[:, eight], values[:, eight], src))
                        if r < n // 8 - 1:
                            settle()
                            did(nc.vector.match_replace(src, values[:, eight], src, -1.0))
                            settle()

                did(nc.vector.tensor_copy(left[:], g.aff_rows[:, PROMPT:]))
                pick(g.aff_rows[:, 0:PROMPT], top_p, at_p, CAP_P)
                settle()
                pick(left[:], top, at, CAP_L)
                settle()
                did(nc.vector.tensor_copy(at_pf[:], at_p[:]), picked)
                did(nc.vector.tensor_copy(at_f[:], at[:]), picked)
                settle()
                did(nc.vector.tensor_scalar(at_f[:], at_f[:], float(PROMPT), None, ALU.add), picked)
                did(nc.vector.tensor_copy(left[:, 0:1], at_pf[:, 0:1]), picked)
                dve.wait_ge(slots_turned, 1)
                did(nc.vector.tensor_copy(g.slot_gate[:], ps[0][:, 0:E]))
                did(nc.vector.tensor_copy(g.slot_row[:, 0:E], ps[1][:, 0:E]))
                did(nc.vector.tensor_copy(g.slot_gate_p[:], ps[2][0:CAP_P, 0:E]))
                did(nc.vector.tensor_copy(g.slot_row_p[:, 0:E], ps[3][0:CAP_P, 0:E]))
                settle()


def experts(nc, g):
    N = CAP_L + CAP_P
    ctx = ExitStack()
    with ctx:
        def sb(name, shape):
            return ctx.enter_context(nc.sbuf_tensor(name, shape, F32))

        xe, xe_p = sb("xe", [P, D]), sb("xe_p", [CAP_P, D])
        xeT = sb("xeT", [P, DT, N])
        silu = sb("silu", [P, 2, N])
        hT = sb("hidT", [P, FT, N])
        yT = sb("yT", [P, DT, N])
        ye, ye_p = sb("ye", [P, D]), sb("ye_p", [CAP_P, D])
        free_mark = sb("free_mark", [1, 1])
        ps_ab = [ctx.enter_context(nc.psum_tensor(f"ps_ab{i}", [P, 512], F32)) for i in range(2)]
        ps_yy = [ctx.enter_context(nc.psum_tensor(f"ps_yy{i}", [P, 512], F32)) for i in range(2)]
        ps_t = [ctx.enter_context(nc.psum_tensor(f"ps_t{i}", [P, 512], F32)) for i in range(4)]
        sem = g.sem
        h_kept, yT_kept, ye_kept, ye_free = sem("h_kept"), sem("yT_kept"), sem("ye_kept"), sem("ye_free")
        gathered, scattered, silu_ready = sem("gathered"), sem("scattered"), sem("silu_ready")
        ab_summed, y_done = g.ab_summed, g.y_done
        xe_turned, xT_act, xT_dve = sem("xe_turned"), sem("xT_act"), sem("xT_dve")
        y_turned = sem("y_turned")

        with nc.Block() as block:
            @block.sync
            def _(sp):
                for p in range(g.RING // 2, 8):
                    g.load_pair(sp, 0, p)
                for q in range(8):
                    g.load_w2(sp, 0, q)
                with sp.Fori(1, E) as e:
                    for p in range(8):
                        g.load_pair(sp, e, p)
                    for q in range(8):
                        g.load_w2(sp, e, q)

            @block.gpsimd
            def _(pool):
                def gather(e):
                    nc.gpsimd.indirect_dma_start(xe[:], None, g.normed, bass.IndirectOffsetOnAxis(ap=g.slot_row[:, e:e + 1], axis=0)).then_inc(gathered, 16)
                    nc.gpsimd.indirect_dma_start(xe_p[:], None, g.normed, bass.IndirectOffsetOnAxis(ap=g.slot_row_p[:, e:e + 1], axis=0)).then_inc(gathered, 16)

                nc.gpsimd.memset(free_mark[:], 0.0).then_inc(ye_free, 1)
                gather(0)
                for e in range(E):
                    pool.wait_ge(xe_turned, e + 1)
                    pool.wait_ge(gathered, 32 * (e + 1))
                    gather(min(e + 1, E - 1))
                    pool.wait_ge(ye_kept, 4 * (e + 1) + 1)
                    nc.gpsimd.indirect_dma_start(g.stream, bass.IndirectOffsetOnAxis(ap=g.slot_row[:, e:e + 1], axis=0), ye[:], None,
                                                 compute_op=ALU.add).then_inc(scattered, 16)
                    nc.gpsimd.indirect_dma_start(g.stream, bass.IndirectOffsetOnAxis(ap=g.slot_row_p[:, e:e + 1], axis=0), ye_p[:], None,
                                                 compute_op=ALU.add).then_inc(scattered, 16)
                    pool.wait_ge(scattered, 32 * (e + 1))
                    nc.gpsimd.memset(free_mark[:], 0.0).then_inc(ye_free, 1)

            @block.scalar
            def _(act):
                did = g.act.did

                def keep_x():
                    for k in range(4):
                        src = ps_t[k // 2][:, N * (k % 2):N * (k % 2) + N]
                        for grp, cols in ((1, slice(0, CAP_L)), (0, slice(CAP_L, N))):
                            did(nc.scalar.activation(xeT[:, k, cols], src[:, cols], ACT.Identity, scale=g.mod[:, grp, 2, k:k + 1],
                                                     bias=g.mod[:, grp, 3, k:k + 1]), xT_act if k == 3 and grp == 0 else None)

                act.wait_ge(xe_turned, 1)
                keep_x()
                with act.Fori(0, E) as e:
                    for f in range(FT):
                        act.wait_ge(ab_summed, e * FT + (f + 1))
                        act.wait_ge(h_kept, e * FT + (f + 1))
                        nc.scalar.activation(silu[:, f % 2], ps_ab[f % 2][:, 0:N], ACT.Silu).then_inc(silu_ready, 1)
                    act.wait_ge(xe_turned, e + 2)
                    keep_x()
                    for d in range(DT):
                        act.wait_ge(y_done, e * DT + (d + 1))
                        for grp, cols in ((1, slice(0, CAP_L)), (0, slice(CAP_L, N))):
                            ins = nc.scalar.activation(yT[:, d, cols], ps_yy[d % 2][:, cols], ACT.Copy, scale=g.mod[:, grp, 4, d:d + 1])
                            if grp == 0:
                                ins.then_inc(yT_kept, 1)

            @block.tensor
            def _(pe):
                def turn_x():
                    for k in range(DT):
                        nc.tensor.transpose(ps_t[k // 2][:, N * (k % 2):N * (k % 2) + CAP_L], xe[:, bass.ts(k, P)], g.ident)
                        mm = nc.tensor.transpose(ps_t[k // 2][:, N * (k % 2) + CAP_L:N * (k % 2) + N], xe_p[:, bass.ts(k, P)], g.ident[0:CAP_P, 0:CAP_P])
                    mm.then_inc(xe_turned, 1)

                pe.wait_ge(gathered, 32)
                turn_x()
                pe.wait_ge(h_kept, 2)
                pe.wait_ge(yT_kept, 2)
                with pe.Fori(0, E) as e:
                    pe.wait_ge(xT_act, e + 1)
                    pe.wait_ge(xT_dve, e + 1)
                    for f in range(FT):
                        pe.wait_ge(h_kept, e * FT + (f + 1))
                        p, c = divmod(f, 2)
                        for w in range(2):
                            s, turn = g.slot(2 * p + w)
                            if c == 0:
                                pe.wait_ge(g.slot_loaded[s], e * 32 + 16 * (turn + 1))
                            unit = g.ring[:, s].rearrange("p (k n) -> p k n", k=DT)
                            for k in range(DT):
                                mm = nc.tensor.matmul(ps_ab[f % 2][:, N * w:N * w + N], unit[:, k, bass.ts(c, P)], xeT[:, k],
                                                      start=(k == 0), stop=(k == DT - 1))
                        mm.then_inc(ab_summed, 1)
                    pe.wait_ge(ye_kept, e * 4 + 1)
                    pe.wait_ge(gathered, e * 32 + 64)
                    turn_x()
                    pe.wait_ge(h_kept, e * FT + (FT + 2))
                    for d in range(DT):
                        pe.wait_ge(yT_kept, e * DT + (d + 1))
                        for f in range(FT):
                            s, turn = g.slot(16 + f // 2)
                            if d == 0 and f % 2 == 0:
                                pe.wait_ge(g.slot_loaded[s], e * 32 + 16 * (turn + 1))
                            unit = g.ring[:, s].rearrange("p (c n) -> p c n", c=2)
                            mm = nc.tensor.matmul(ps_yy[d % 2][:, 0:N], unit[:, f % 2, bass.ts(d, P)], hT[:, f], start=(f == 0), stop=(f == FT - 1))
                            if d == DT - 1 and f % 2 and f < FT - 1:
                                mm.then_inc(g.w2_used, 1)
                        mm.then_inc(y_done, 1)
                    pe.wait_ge(yT_kept, e * DT + (DT + 2))
                    pe.wait_ge(xT_act, e + 2)
                    pe.wait_ge(xT_dve, e + 2)
                    for h in range(2):
                        for k in range(4):
                            nc.tensor.transpose(ps_t[2 * h][:, bass.ts(k, P)], yT[:, 4 * h + k, 0:CAP_L], g.ident)
                        for k in range(4):
                            mm = nc.tensor.transpose(ps_t[2 * h + 1][0:CAP_P, bass.ts(k, P)], yT[:, 4 * h + k, CAP_L:N], g.ident)
                        mm.then_inc(y_turned, 1)

            @block.vector
            def _(dve):
                did = g.dve.did
                for b in range(2):
                    did(nc.vector.memset(silu[:, b], 0.0), h_kept)
                    did(nc.vector.memset(yT[:, b], 0.0), yT_kept)
                did(nc.vector.memset(ye_p[:], 0.0), ye_kept)
                g.dve.settle()

                def keep_x():
                    for k in range(4, DT):
                        src = ps_t[k // 2][:, N * (k % 2):N * (k % 2) + N]
                        for grp, cols in ((1, slice(0, CAP_L)), (0, slice(CAP_L, N))):
                            ins = nc.vector.tensor_scalar(xeT[:, k, cols], src[:, cols], g.mod[:, grp, 2, k:k + 1], g.mod[:, grp, 3, k:k + 1],
                                                          ALU.mult, ALU.add)
                            if k == DT - 1 and grp == 0:
                                ins.then_inc(xT_dve, 1)

                dve.wait_ge(xe_turned, 1)
                keep_x()
                with dve.Fori(0, E) as e:
                    for f in range(FT):
                        dve.wait_ge(silu_ready, e * FT + (f + 1))
                        nc.vector.tensor_tensor(hT[:, f], silu[:, f % 2], ps_ab[f % 2][:, N:2 * N], ALU.mult).then_inc(h_kept, 1)
                    dve.wait_ge(xe_turned, e + 2)
                    keep_x()
                    for h in range(2):
                        dve.wait_ge(y_turned, e * 2 + (h + 1))
                        if h == 0:
                            dve.wait_ge(ye_free, e + 1)
                        cols = bass.ts(h, 512)
                        nc.vector.tensor_scalar(ye[:, cols], ps_t[2 * h][:], g.slot_gate[:, bass.ds(e, 1)], None, ALU.mult).then_inc(ye_kept, 1)
                        nc.vector.tensor_scalar(ye_p[:, cols], ps_t[2 * h + 1][0:CAP_P, :], g.slot_gate_p[:, bass.ds(e, 1)], None,
                                                ALU.mult).then_inc(ye_kept, 1)


def finish(nc, g):
    ctx = ExitStack()
    with ctx:
        def sb(name, shape):
            return ctx.enter_context(nc.sbuf_tensor(name, shape, F32))

        xs = sb("xs", [P, TILES, D])
        final_g = sb("final_g_row", [P, D])
        squares = ctx.enter_context(nc.sbuf_tensor("squares3", [P, D], mybir.dt.bfloat16))
        ms = sb("ms3", [P, TILES])
        rs = sb("rs3", [P, TILES])
        half = sb("half3", [P, TILES])
        tile_loaded, weights_end = g.slot_loaded, 32 * E
        gain_loaded, summed, inverted, scaled, outputs_stored = (
            g.sem(n) for n in ("gain_loaded", "summed", "inverted", "scaled", "outputs_stored"))

        with nc.Block() as block:
            @block.sync
            def _(sp):
                sp.dma_start(final_g[:], g.final_g.to_broadcast([P, D])).then_inc(gain_loaded, 16)
                for i in range(TILES):
                    sp.dma_start(xs[:, i], g.stream[bass.ts(i, P), :]).then_inc(tile_loaded[i], 16)
                for i in range(TILES):
                    sp.wait_ge(scaled, i + 1)
                    dst = g.y_prompt_out if i == 0 else g.y_latent_out[bass.ts(i - 1, P), :]
                    sp.dma_start(dst, xs[:, i]).then_inc(outputs_stored, 16)
                sp.wait_ge(outputs_stored, 16 * TILES)

            @block.scalar
            def _(act):
                for i in range(TILES):
                    act.wait_ge(tile_loaded[i], weights_end + 16)
                    if i:
                        g.act.settle()
                    g.act.did(nc.scalar.activation(squares[:], xs[:, i], ACT.Square, scale=D ** -0.5, accum_out=ms[:, i:i + 1]), summed)

            @block.gpsimd
            def _(pool):
                for i in range(TILES):
                    pool.wait_ge(summed, i + 1)
                    nc.gpsimd.tensor_tensor(rs[:, i:i + 1], ms[:, i:i + 1], g.eps[:], ALU.add).then_inc(inverted, 1)
                    pool.wait_ge(inverted, 2 * i + 1)
                    nc.gpsimd.tensor_tensor(rs[:, i:i + 1], rs[:, i:i + 1], g.minus_half[:, 0:1], ALU.pow).then_inc(inverted, 1)

            @block.vector
            def _(dve):
                dve.wait_ge(gain_loaded, 16)
                for i in range(TILES):
                    dve.wait_ge(inverted, 2 * i + 2)
                    dve.wait_ge(tile_loaded[i], weights_end + 16)
                    g.dve.did(nc.vector.scalar_tensor_tensor(xs[:, i], xs[:, i], rs[:, i:i + 1], final_g[:], ALU.mult, ALU.mult), scaled)


def constants():
    import numpy as np

    def dft(n):
        a = 2 * np.pi * (np.outer(np.arange(n), np.arange(n)) % n) / n
        return np.cos(a), np.sin(a)

    c64, s64 = dft(GRID_W)
    c128, s128 = dft(P)
    c16, s16 = dft(GRID_H)
    two, eight = np.eye(P // GRID_W), np.eye(8)
    pick_lane = np.zeros((P, LANES, P))
    for r in range(LANES):
        pick_lane[32 * (r // HEADS) + r % HEADS, r] = 1
    pick2 = np.zeros((P, 2, P))
    pick2[0, 0], pick2[1, 1] = 1, 1
    s, l = np.arange(P)[:, None], np.arange(P)[None, :]
    masks = np.stack([np.where(s <= l, 0, MASKED), np.where(s >= l, 0, MASKED)], 1)
    parts = {
        "ident": np.eye(P),
        "dft_cols": np.concatenate([np.kron(two, c64), -np.kron(two, s64)], 1),
        "dft_prompt": np.concatenate([c128, -s128], 1),
        "dft_chan_r": np.concatenate([c128, -s128], 1),
        "dft_chan_i": np.concatenate([s128, c128], 1),
        "dft_row_c": np.kron(c16, eight),
        "dft_row_s": np.kron(s16, eight),
        "pick_lane": pick_lane.reshape(P, -1),
        "pick2": pick2.reshape(P, -1),
        "masks": masks.reshape(P, -1),
    }
    spans, at = {}, 0
    for name, a in parts.items():
        spans[name] = (at, at + a.shape[1])
        at += a.shape[1]
    return np.concatenate(list(parts.values()), 1).astype(np.float32), spans


def weight_loads(g):
    w1, w3 = (w.rearrange("e (k p) f -> e p k f", p=P) for w in (g.exp_w1, g.exp_w3))
    w2 = g.exp_w2.rearrange("e (q c p) d -> e q p c d", c=2, p=P)

    def slot(j):
        return j % g.RING, j // g.RING

    def expert(w, e):
        return w[e] if isinstance(e, int) else w[bass.ds(e, 1)].rearrange("a p k f -> (a p) k f")

    def wait_unit(sp, e, j):
        if j < 0:
            if isinstance(e, int):
                return
            e, j = e - 1, j + 24
        if j < 16:
            sp.wait_ge(g.ab_summed, e * FT + 2 * (j // 2 + 1))
        elif j < 23:
            sp.wait_ge(g.w2_used, e * 7 + (j - 15))
        else:
            sp.wait_ge(g.y_done, e * DT + DT)

    def load_pair(sp, e, p):
        for n, w in enumerate((w1, w3)):
            s, _ = slot(2 * p + n)
            wait_unit(sp, e, 2 * p + n - g.RING)
            sp.dma_start(g.ring[:, s].rearrange("p (k n) -> p k n", k=DT), expert(w, e)[:, :, bass.ts(p, 256)]).then_inc(g.slot_loaded[s], 16)

    def load_w2(sp, e, q):
        s, _ = slot(16 + q)
        wait_unit(sp, e, 16 + q - g.RING)
        src = w2[e, q] if isinstance(e, int) else w2[bass.ds(e, 1), q].rearrange("a p c d -> (a p) c d")
        sp.dma_start(g.ring[:, s].rearrange("p (c n) -> p c n", c=2), src).then_inc(g.slot_loaded[s], 16)

    g.slot, g.load_pair, g.load_w2 = slot, load_pair, load_w2


def build(nc, t, spans):
    ctx = ExitStack()
    g = Shared()
    g.x_prompt, g.x_latent, g.state_C = t["x_prompt"], t["x_latent"], t["state_C"]
    g.state_n, g.state_m, g.c = t["state_n"], t["state_m"], t["c"]
    g.c_ctx, g.ada_w, g.ada_b = t["c_ctx"], t["ada_w"], t["ada_b"]
    g.norm1_g, g.norm2_g, g.w_in = t["norm1_g"], t["norm2_g"], t["w_in"]
    g.b_in, g.head_g, g.w_out = t["b_in"], t["head_g"], t["w_out"]
    g.router_w, g.exp_w1, g.exp_w3 = t["router_w"], t["exp_w1"], t["exp_w3"]
    g.exp_w2, g.final_g, g.constants = t["exp_w2"], t["final_g"], t["constants"]
    g.y_prompt_out, g.y_latent_out, g.new_C = t["y_prompt_out"], t["y_latent_out"], t["new_C"]
    g.new_n, g.new_m = t["new_n"], t["new_m"]
    with ctx:
        def sb(name, shape, stack=ctx, dt=F32):
            return stack.enter_context(nc.sbuf_tensor(name, shape, dt))

        def sem(name):
            return ctx.enter_context(nc.semaphore(name))

        def dram(name, shape):
            return nc.dram_tensor(name, shape, F32, kind="Internal").ap()

        g.sem = sem
        g.act = Steps(nc.scalar, sem("act_steps"))
        g.dve = Steps(nc.vector, sem("dve_steps"))
        g.kvo = dram("kvo", [ROWS, 3 * WIDTH])
        g.qkT = dram("qkT_dram", [ROWS, 2 * WIDTH])
        g.stream = dram("stream", [ROWS, D])
        g.normed = dram("normed", [ROWS, D])
        g.ada_b_row = g.ada_b.rearrange("a b -> (a b)")[None, :]
        g.b_in_col = g.b_in.rearrange("a b -> (a b)")[:, None]
        g.w_in_src = g.w_in.rearrange("(k p) n -> p k n", p=P)
        g.w_out_src = g.w_out.rearrange("(k p) n -> p k n", p=P)
        g.x_rows = lambda i: g.x_prompt if isinstance(i, int) and i == 0 else g.x_latent[bass.ts(i - 1, P), :]

        g.const = sb("const", [P, max(b for _, b in spans.values())])
        part = {name: g.const[:, a:b] for name, (a, b) in spans.items()}
        g.ident, g.dft_cols, g.dft_prompt, g.dft_chan_r, g.dft_chan_i = (
            part["ident"], part["dft_cols"], part["dft_prompt"], part["dft_chan_r"], part["dft_chan_i"])
        g.dft_row_c, g.dft_row_s, g.pick_lane, g.pick2, g.masks = (
            part["dft_row_c"], part["dft_row_s"], part["pick_lane"], part["pick2"], part["masks"])
        g.mod = sb("mod", [P, 2, 5, DT])
        g.gate1 = sb("gate1", [P, 2, D])
        g.minus_half = sb("minus_half", [P, HEADS])
        g.eps = sb("eps", [P, 1])
        g.aff_rows = sb("aff_rows", [E, ROWS])
        g.w_in_loaded = sem("w_in_loaded")
        g.w_out_loaded = sem("w_out_loaded")
        with ExitStack() as mixer:
            g.cols = sb("cols", [P, 4, TILES, LANES], mixer)
            shared = sb("m_rows", [P, ROWS], mixer)
            g.shared_rows = shared
            g.m_row = shared[0:64, :]
            g.w_gate = shared[:, 0:D].rearrange("p (k n) -> p k n", k=DT)
            with ExitStack() as heads:
                g.y = sb("y", [P, 4, 2, LATENT], heads)[:]
                g.y_prompt = sb("y_prompt", [P, 4, 2, PROMPT], heads)
                g.gate_rows = sb("gate_rows", [P, ROWS], heads)
                with ExitStack() as weights:
                    g.w_in_sb = sb("w_in_sb", [P, DT, IN_COLS], weights)
                    g.b_in_row = sb("b_in_row", [P, IN_COLS], weights)
                    modulation(nc, g)
                    projection(nc, g)
                g.states = sb("states", [P, TILES, LANES, VW], heads)
                g.fuT = sb("fuT", [P, 4, ROWS], heads)
                recurrence(nc, g)
                g.w_out_sb = g.y.rearrange("p a b n -> p (a b n)").rearrange("p (k n) -> p k n", k=DT)
                mixing(nc, g)
        g.slot_gate, g.slot_gate_p = sb("slot_gate", [P, E]), sb("slot_gate_p", [CAP_P, E])
        g.slot_row, g.slot_row_p = sb("slot_row", [P, E], dt=U32), sb("slot_row_p", [CAP_P, E], dt=U32)
        g.RING = 12
        with ExitStack() as weights:
            g.ring = sb("ring", [P, g.RING, 2 * D], weights)
            g.slot_loaded = [sem(f"slot_loaded{i}") for i in range(g.RING)]
            g.ab_summed, g.w2_used, g.y_done = sem("ab_summed"), sem("w2_used"), sem("y_done")
            weight_loads(g)
            routing(nc, g)
            experts(nc, g)
        finish(nc, g)


_INPUTS = {
    "x_prompt": ("x_prompt", (PROMPT, D)), "x_latent": ("x_sample", (LATENT, D)),
    "state_C": ("state_C", (LANES * HD, HD)), "state_n": ("state_n", (LANES, HD)), "state_m": ("state_m", (LANES, 1)),
    "c": ("c", (DT, P)), "c_ctx": ("c_ctx", (DT, P)), "ada_w": ("ada_w", (D, MOD_COLS)), "ada_b": ("ada_b", (MOD_T, P)),
    "norm1_g": ("norm1_g", (DT, P)), "norm2_g": ("norm2_g", (DT, P)), "w_in": ("w_in", (D, IN_COLS)), "b_in": ("b_in", (1, IN_COLS)),
    "head_g": ("head_g", (1, WIDTH)), "w_out": ("w_out", (D, D)), "router_w": ("router_w", (D, E)),
    "exp_w1": ("exp_w1", (E, D, F)), "exp_w3": ("exp_w3", (E, D, F)), "exp_w2": ("exp_w2", (E, F, D)), "final_g": ("final_g", (1, D)),
}
_OUTPUTS = {
    "y_prompt_out": (PROMPT, D), "y_latent_out": (LATENT, D),
    "new_C": (LANES * HD, HD), "new_n": (LANES, HD), "new_m": (LANES, 1),
}


def kernel(**inputs):
    import numpy as np
    import concourse.bacc as bacc
    from concourse.bass_utils import run_bass_kernel_spmd

    nc = bacc.Bacc("TRN2", target_bir_lowering=False, num_devices=1)
    table, spans = constants()
    arrays = {name: np.ascontiguousarray(np.asarray(inputs[key]).reshape(shape)) for name, (key, shape) in _INPUTS.items()}
    arrays["constants"] = table
    t = {name: nc.dram_tensor(f"in_{name}", a.shape, mybir.dt.from_np(a.dtype), kind="ExternalInput").ap()
         for name, a in arrays.items()}
    for name, shape in _OUTPUTS.items():
        t[name] = nc.dram_tensor(f"out_{name}", shape, F32, kind="ExternalOutput").ap()
    build(nc, t, spans)
    r = run_bass_kernel_spmd(nc, [{f"in_{name}": a for name, a in arrays.items()}], core_ids=[0]).results[0]
    return (
        r["out_y_prompt_out"].reshape(1, PROMPT, D),
        r["out_y_latent_out"].reshape(1, LATENT, D),
        r["out_new_C"].reshape(1, 1, 2, HEADS, HD, HD),
        r["out_new_n"].reshape(1, 1, 2, HEADS, HD),
        r["out_new_m"].reshape(1, 1, 2, HEADS),
    )
```

```python
from contextlib import ExitStack, contextmanager

import concourse.bass as bass
from concourse import mybir
from concourse.alu_op_type import AluOpType as ALU

ACT = mybir.ActivationFunctionType
AX = mybir.AxisListType
F32 = mybir.dt.float32
U32 = mybir.dt.uint32

P = 128
D = 1024
DT = D // P
PROMPT, LATENT = 128, 1024
ROWS = PROMPT + LATENT
TILES = ROWS // P
GRID_W = 64
GRID_H = LATENT // GRID_W
HEADS = 4
WIDTH = 512
HD = WIDTH // HEADS
LANES = 2 * HEADS
N_GATES = 4 * HEADS
OFF_G = 4 * WIDTH
OFF_F = OFF_G + N_GATES
IN_COLS = OFF_F + WIDTH
E = 16
F = 2 * D
FT = F // P
CAP_L = 2 * LATENT // E
CAP_P = 2 * PROMPT // E
N_MOD = 6
MOD_COLS = N_MOD * D
MOD_T = MOD_COLS // P
EPS = 1e-6
K_SCALE = HD ** -0.5
HUGE = 3.0e38
MASKED = 1.0e30
VW = HD + 1
SECOND = 32
HALVES = SECOND + E


class Shared:
    pass


class Steps:

    def __init__(self, engine, own):
        self.engine, self.own = engine, own
        self.count, self.added, self.latest = {}, {}, None

    def did(self, instruction, sem=None):
        sem = sem or self.own
        instruction.then_inc(sem, 1)
        self.count[sem.name] = self.count.get(sem.name, 0) + 1
        self.added[sem.name] = self.added.get(sem.name, 0) + 1
        self.latest = sem

    def mark(self):
        return self.latest, self.count[self.latest.name]

    def settle(self, mark=None):
        self.engine.wait_ge(*(mark or self.mark()))

    @contextmanager
    def loop(self, engine, times, per):
        with engine.Fori(0, times) as j:
            start = {n: self.count.get(n, 0) for n in per}
            self.count.update({n: j * per[n] + start[n] for n in per})
            self.added = {}
            yield j
            assert self.added == per, self.added
        self.count.update({n: start[n] + times * per[n] for n in per})


def modulation(nc, g):
    NB, RING = MOD_COLS // 512, 3
    ctx = ExitStack()
    with ctx:
        def sb(name, shape):
            return ctx.enter_context(nc.sbuf_tensor(name, shape, F32))

        vec_rows = sb("vec_rows", [32, P])
        bias_rows = sb("bias_rows", [MOD_T, P])
        held = g.y.rearrange("p a b n -> p (a b n)").rearrange("p (s k n) -> p s k n", s=2, k=DT)
        last = g.w_in_sb[:, DT - 2:].rearrange("p k n -> p (k n)")[:, 0:DT * 512].rearrange("p (k n) -> p k n", k=DT)
        ada = [held[:, 0], held[:, 1], last]
        mod_row = sb("mod_row", [2, MOD_COLS])
        vecT = sb("vecT", [P, 32])
        biasT = sb("biasT", [P, MOD_T])
        modT = sb("modT", [P, MOD_T, 2])
        gate1_bias = sb("gate1_bias", [P, D])
        ps_row = [ctx.enter_context(nc.psum_tensor(f"ps_row{i}", [P, 512], F32)) for i in range(RING)]
        ps_col = ctx.enter_context(nc.psum_tensor("ps_col", [P, 512], F32))
        ps_gate = [ctx.enter_context(nc.psum_tensor(f"ps_gate{i}", [P, 512], F32)) for i in range(4)]

        small_loaded, rest_loaded, minus_half_set = g.sem("small_loaded"), g.sem("rest_loaded"), g.sem("minus_half_set")
        ada_loaded = [g.sem(f"ada_loaded{i}") for i in range(RING)]
        silu_done = g.sem("silu_done")
        vec_turned = g.sem("vec_turned")
        vec_kept = g.sem("vec_kept")
        row_summed = g.sem("row_summed")
        row_kept = g.sem("row_kept")
        mod_turned = g.sem("mod_turned")
        gate_spread = g.sem("gate_spread")
        ada_src = g.ada_w.rearrange("(k p) n -> p k n", p=P)

        with nc.Block() as block:
            @block.sync
            def _(sp):
                sp.dma_start(vec_rows[0:8, :], g.c_ctx).then_inc(small_loaded, 16)
                sp.dma_start(vec_rows[8:16, :], g.c).then_inc(small_loaded, 16)
                sp.dma_start(vec_rows[16:24, :], g.norm1_g).then_inc(small_loaded, 16)
                sp.dma_start(vec_rows[24:32, :], g.norm2_g).then_inc(small_loaded, 16)
                sp.dma_start(bias_rows[:], g.ada_b).then_inc(small_loaded, 16)
                sp.dma_start(g.const[:, 0:P], g.constants[:, 0:P]).then_inc(small_loaded, 16)

                def load(n, s, reused):
                    if reused:
                        sp.wait_ge(row_summed, n - RING + 1)
                    sp.dma_start(ada[s], ada_src[:, :, bass.ts(n, 512)]).then_inc(ada_loaded[s], 16)

                for n in range(RING):
                    load(n, n, False)
                sp.dma_start(g.const[:, P:], g.constants[:, P:]).then_inc(rest_loaded, 16)
                sp.dma_start(gate1_bias[:], g.ada_b_row[:, 2 * D:3 * D].to_broadcast([P, D])).then_inc(rest_loaded, 16)
                for i in range(2):
                    sp.dma_start(g.xt[:, i], g.x_rows(i)).then_inc(g.x_loaded[i], 16)
                with sp.Fori(1, NB // RING) as j:
                    for s in range(RING):
                        load(j * RING + s, s, True)
                for n in range(4):
                    if n == 3:
                        sp.wait_ge(row_summed, NB)
                    sp.dma_start(g.w_in_sb[:, 2 * n:2 * n + 2], g.w_in_src[:, 2 * n:2 * n + 2]).then_inc(g.w_in_loaded, 16)
                sp.dma_start(g.b_in_row[:], g.b_in.to_broadcast([P, IN_COLS])).then_inc(g.b_in_loaded, 16)

            @block.scalar
            def _(act):
                act.wait_ge(small_loaded, 16 * 6)
                g.act.did(nc.scalar.activation(vec_rows[0:16, :], vec_rows[0:16, :], ACT.Silu), silu_done)
                mean_square(nc, g, act, 0, 0, 0)

            @block.gpsimd
            def _(pool):
                pool.wait_ge(minus_half_set, 1)
                invert_rms(nc, g, pool, 0, 0)

            @block.tensor
            def _(pe):
                pe.wait_ge(silu_done, 1)
                nc.tensor.transpose(ps_col[:, 0:32], vec_rows[:], g.ident[0:32, 0:32])
                nc.tensor.transpose(ps_col[:, 32:32 + MOD_T], bias_rows[:], g.ident[0:MOD_T, 0:MOD_T]).then_inc(vec_turned, 1)
                pe.wait_ge(vec_kept, 2)

                def block_sum(n, s, half, reused):
                    pe.wait_ge(ada_loaded[s], 16 * (half + 1))
                    if reused:
                        pe.wait_ge(row_kept, n - RING + 1)
                    for k in range(DT):
                        mm = nc.tensor.matmul(ps_row[s][0:2, :], vecT[:, k:16:DT], ada[s][:, k, :],
                                              start=(k == 0), stop=(k == DT - 1))
                    mm.then_inc(row_summed, 1)

                for n in range(RING):
                    block_sum(n, n, 0, False)
                with pe.Fori(1, NB // RING) as j:
                    for s in range(RING):
                        block_sum(j * RING + s, s, j, True)
                pe.wait_ge(row_kept, NB)
                pe.wait_ge(rest_loaded, 32)
                for n in range(4):
                    grp, h = divmod(n, 2)
                    mm = nc.tensor.matmul(ps_gate[n][:], g.pick2[0:2, bass.ts(grp, P)],
                                          mod_row[:, 2 * D + 512 * h:2 * D + 512 * h + 512], start=True, stop=True)
                mm.then_inc(gate_spread, 1)
                for t in range(MOD_T):
                    mm = nc.tensor.transpose(ps_col[:, 2 * t:2 * t + 2], mod_row[:, bass.ts(t, P)], g.ident[0:2, 0:2])
                mm.then_inc(mod_turned, 1)

            @block.vector
            def _(dve):
                g.dve.did(nc.vector.memset(g.minus_half[:], -0.5), minus_half_set)
                dve.wait_ge(vec_turned, 1)
                g.dve.did(nc.vector.tensor_copy(vecT[:], ps_col[:, 0:32]), vec_kept)
                g.dve.did(nc.vector.tensor_copy(biasT[:], ps_col[:, 32:32 + MOD_T]), vec_kept)

                def keep(n, s):
                    dve.wait_ge(row_summed, n + 1)
                    g.dve.did(nc.vector.tensor_copy(mod_row[:, bass.ts(n, 512)], ps_row[s][0:2, :]), row_kept)

                with g.dve.loop(dve, NB // RING, {"row_kept": RING}) as j:
                    for s in range(RING):
                        keep(j * RING + s, s)
                normed(nc, g, dve, 0, 0, 0)
                dve.wait_ge(rest_loaded, 32)
                dve.wait_ge(gate_spread, 1)
                for n in range(4):
                    grp, h = divmod(n, 2)
                    g.dve.did(nc.vector.tensor_tensor(g.gate1[:, grp, bass.ts(h, 512)], ps_gate[n][:],
                                                      gate1_bias[:, bass.ts(h, 512)], ALU.add))
                dve.wait_ge(mod_turned, 1)
                g.dve.did(nc.vector.tensor_tensor(modT[:], ps_col[:, 0:2 * MOD_T].rearrange("p (t c) -> p t c", c=2),
                                                  biasT[:, :, None].to_broadcast([P, MOD_T, 2]), ALU.add))
                g.dve.settle()
                for grp in range(2):
                    for scale, shift, gain, off in ((1, 0, 16, 0), (4, 3, 24, 2)):
                        g.dve.did(nc.vector.scalar_tensor_tensor(
                            g.mod[:, grp, off], modT[:, scale * DT:(scale + 1) * DT, grp], 1.0, vecT[:, gain:gain + DT],
                            ALU.add, ALU.mult))
                        g.dve.did(nc.vector.tensor_copy(g.mod[:, grp, off + 1], modT[:, shift * DT:(shift + 1) * DT, grp]))
                    g.dve.did(nc.vector.tensor_copy(g.mod[:, grp, 4], modT[:, 5 * DT:6 * DT, grp]))
                g.dve.settle()


def tile_loop(engine, steps, body, per=None):
    body(0, 0, 0)
    body(1, 1, 0)
    if steps is None:
        with engine.Fori(1, TILES // 2) as j:
            body(j * 2, 0, j)
            body(j * 2 + 1, 1, j)
    else:
        with steps.loop(engine, TILES // 2 - 1, per) as j:
            body(j * 2 + 2, 0, j + 1)
            body(j * 2 + 3, 1, j + 1)
    body(TILES - 1, 0, TILES // 2)


def first(i):
    return isinstance(i, int) and i < 2


def mean_square(nc, g, act, i, par, half):
    act.wait_ge(g.x_loaded[par], 16 * (half + 1))
    if not first(i):
        act.wait_ge(g.rms_inverted, i - 1)
    g.act.settle()
    g.act.did(nc.scalar.activation(g.squares[:], g.xt[:, par], ACT.Square, accum_out=g.ms[:, par, 0:1]), g.squares_summed)
    g.act.settle()
    g.act.did(nc.scalar.activation(g.ms[:, par, 1:2], g.ms[:, par, 0:1], ACT.Copy, bias=EPS, scale=1.0 / D), g.squares_summed)


def invert_rms(nc, g, pool, i, par):
    pool.wait_ge(g.squares_summed, 2 * i + 2)
    nc.gpsimd.tensor_tensor(g.ms[:, par, 2:3], g.ms[:, par, 1:2], g.minus_half[:, 0:1], ALU.pow).then_inc(g.rms_inverted, 1)


def normed(nc, g, dve, i, par, half):
    dve.wait_ge(g.rms_inverted, i + 1)
    dve.wait_ge(g.x_loaded[par], 16 * (half + 1))
    if not (isinstance(i, int) and i == 0):
        dve.wait_ge(g.x_turned, 2 * i)
    g.dve.did(nc.vector.tensor_scalar(g.xn[:], g.xt[:, par], g.ms[:, par, 2:3], None, ALU.mult), g.x_normed)


def projection(nc, g):
    ctx = ExitStack()
    with ctx:
        def sb(name, shape):
            return ctx.enter_context(nc.sbuf_tensor(name, shape, F32))

        xt, xn = g.xt, g.xn
        hT = sb("hT", [P, 2, DT, P])
        pr = sb("pr", [P, 2, 5, 512])
        qkT = sb("qkT", [P, 2 * HEADS, P])
        w_gate = g.w_gate
        b_gate = sb("b_gate", [P, 1])

        def bank(name):
            return ctx.enter_context(nc.psum_tensor(name, [P, 512], F32))

        ps_x = [bank(f"ps_x{i}") for i in range(2)]
        ps_p = [bank(f"ps_p{i}") for i in range(2)]
        ps_qk = [bank(f"ps_qk{i}") for i in range(2)]
        ps_g = bank("ps_g")
        ps_y = bank("ps_y")
        sem = g.sem
        x_loaded = g.x_loaded
        bg_loaded = sem("bg_loaded")
        weights_set = sem("weights_set")
        x_normed, x_turned = g.x_normed, g.x_turned
        hT_ready_dve, hT_ready_act = sem("hT_ready_dve"), sem("hT_ready_act")
        block_summed = sem("block_summed")
        block_kept = sem("block_kept")
        qk_turned = sem("qk_turned")
        qk_kept = sem("qk_kept")
        gates_summed = sem("gates_summed")
        gates_kept = sem("gates_kept")
        y_summed = sem("y_summed")
        y_kept = sem("y_kept")
        kvo_stored = [sem(f"kvo_stored{i}") for i in range(2)]
        qk_stored = sem("qk_stored")
        COLS = (0, WIDTH, 2 * WIDTH, 3 * WIDTH, OFF_F)

        with nc.Block() as block:
            @block.sync
            def _(sp):
                with_bias = nc.allow_non_contiguous_dma("sixteen gate biases, one per partition")
                with with_bias:
                    for j, c in enumerate((0, 2, 1, 3)):
                        sp.dma_start(b_gate[32 * j:32 * j + HEADS, :],
                                     g.b_in_col[OFF_G + HEADS * c:OFF_G + HEADS * (c + 1), :]).then_inc(bg_loaded, 16)

                def load(i, par):
                    sp.dma_start(xt[:, par], g.x_rows(i)).then_inc(x_loaded[par], 16)

                def store(i, par):
                    sp.wait_ge(block_kept, 5 * i + 4)
                    sp.dma_start(g.kvo[bass.ts(i, P), :], pr[:, par, 1:4].rearrange("p b n -> p (b n)")).then_inc(kvo_stored[par], 16)
                    sp.wait_ge(qk_kept, 2 * i + 2)
                    sp.dma_start(g.qkT[bass.ts(i, P), :], qkT[:].rearrange("p h n -> p (h n)")).then_inc(qk_stored, 16)

                def body(i, par, half):
                    store(i, par)
                    if not (isinstance(i, int) and i + 2 >= TILES):
                        sp.wait_ge(x_normed, i + 1)
                        load(i + 2, par)

                for i in range(2):
                    body(i, i % 2, 0)
                with sp.Fori(1, 3) as j:
                    for par in range(2):
                        body(j * 2 + par, par, j)
                for i in range(6, TILES):
                    body(i, i % 2, 0)
                sp.wait_ge(kvo_stored[0], 16 * 5)
                sp.wait_ge(kvo_stored[1], 16 * 4)
                sp.wait_ge(qk_stored, 16 * TILES)

            @block.gpsimd
            def _(pool):
                def body(i, par, half):
                    if not (isinstance(i, int) and i == 0):
                        invert_rms(nc, g, pool, i, par)

                tile_loop(pool, None, body)

            @block.scalar
            def _(act):
                def keep_h(i, par):
                    grp = 0 if isinstance(i, int) and i == 0 else 1
                    act.wait_ge(x_turned, 2 * i + 2)
                    if not first(i):
                        act.wait_ge(y_summed, 2 * i - 2)
                    for k in range(4, DT):
                        g.act.did(nc.scalar.activation(hT[:, par, k], ps_x[1][:, bass.ts(k - 4, P)], ACT.Identity,
                                                       scale=g.mod[:, grp, 0, k:k + 1], bias=g.mod[:, grp, 1, k:k + 1]), hT_ready_act)

                def keep_y(i):
                    for j in range(2):
                        act.wait_ge(y_summed, 2 * i + j + 1)
                        if isinstance(i, int) and i == 0:
                            src = ps_y[:].rearrange("p (a c n) -> p a c n", a=2, n=P)
                            g.act.did(nc.scalar.activation(g.y_prompt[:, 2 * j:2 * j + 2], src, ACT.Copy), y_kept)
                            continue
                        for row in range(2):
                            src = ps_y[:].rearrange("p (ac r b c) -> p ac r b c", ac=4, r=2, b=8)[:, :, row]
                            dst = g.y[:, 2 * j:2 * j + 2].rearrange("p a c (b n) -> p (a c) b n", b=8)
                            dst = dst[:, :, :, bass.ds(i * 16 + (8 * row - 16), 8)]
                            g.act.did(nc.scalar.activation(dst, src, ACT.Copy), y_kept if row else None)

                def body(i, par, half):
                    if not (isinstance(i, int) and i == TILES - 1):
                        mean_square(nc, g, act, i + 1, 1 - par, half + par)
                    if not (isinstance(i, int) and i == 0):
                        keep_y(i - 1)
                    if not (isinstance(i, int) and i == 0):
                        act.wait_ge(qk_stored, 16 * i)
                    for j in range(2):
                        act.wait_ge(qk_turned, 2 * i + j + 1)
                        g.act.did(nc.scalar.activation(qkT[:, 4 * j:4 * j + 4], ps_qk[j][:].rearrange("p (h n) -> p h n", n=P),
                                                       ACT.Copy, scale=(1.0, K_SCALE)[j]), qk_kept)
                    if not (isinstance(i, int) and i == TILES - 1):
                        keep_h(i + 1, 1 - par)

                keep_h(0, 0)
                tile_loop(act, g.act, body, {"squares_summed": 4, "hT_ready_act": 8, "qk_kept": 4, "y_kept": 4, "act_steps": 4})
                keep_y(TILES - 1)

            @block.tensor
            def _(pe):
                def turn_x(i):
                    pe.wait_ge(x_normed, i + 1)
                    if not (isinstance(i, int) and i == 0):
                        pe.wait_ge(hT_ready_dve, 4 * i)
                        pe.wait_ge(hT_ready_act, 4 * i)
                    for h in range(2):
                        for k in range(4):
                            mm = nc.tensor.transpose(ps_x[h][:, bass.ts(k, P)], xn[:, bass.ts(4 * h + k, P)], g.ident)
                        mm.then_inc(x_turned, 1)

                turn_x(0)

                def body(i, par, half):
                    pe.wait_ge(hT_ready_dve, 4 * i + 4)
                    pe.wait_ge(hT_ready_act, 4 * i + 4)

                    def block_sum(b):
                        if b < 2 and isinstance(i, int) and i == 0:
                            pe.wait_ge(g.w_in_loaded, 16 * 4)
                        else:
                            pe.wait_ge(block_kept, 5 * i + b - 1)
                        for k in range(DT):
                            mm = nc.tensor.matmul(ps_p[(par + b) % 2][:], hT[:, par, k], g.w_in_sb[:, k, COLS[b]:COLS[b] + 512],
                                                  start=(k == 0), stop=(k == DT - 1))
                        mm.then_inc(block_summed, 1)

                    def turn(j):
                        pe.wait_ge(block_kept, 5 * i + j + 1)
                        if not (isinstance(i, int) and i == 0):
                            pe.wait_ge(qk_kept, 2 * i + j - 1)
                        for h in range(HEADS):
                            mm = nc.tensor.transpose(ps_qk[j][:, bass.ts(h, P)], pr[:, par, j, bass.ts(h, P)], g.ident)
                        mm.then_inc(qk_turned, 1)

                    block_sum(0)
                    if not (isinstance(i, int) and i == 0):
                        dft_cols(i - 1, 1 - par, 0)
                    block_sum(1)
                    if not (isinstance(i, int) and i == 0):
                        dft_cols(i - 1, 1 - par, 1)
                    turn(0)
                    block_sum(2)
                    turn(1)
                    block_sum(3)
                    if not (isinstance(i, int) and i == TILES - 1):
                        turn_x(i + 1)
                    block_sum(4)
                    if isinstance(i, int) and i == 0:
                        pe.wait_ge(weights_set, 1)
                    else:
                        pe.wait_ge(gates_kept, i)
                    for k in range(DT):
                        mm = nc.tensor.matmul(ps_g[:, 0:P], w_gate[:, k], hT[:, par, k], start=(k == 0), stop=(k == DT - 1))
                    mm.then_inc(gates_summed, 1)

                def dft_cols(i, par, j):
                    basis = g.dft_prompt if isinstance(i, int) and i == 0 else g.dft_cols
                    if j == 0:
                        pe.wait_ge(block_kept, 5 * i + 5)
                    if not (j == 0 and isinstance(i, int) and i == 0):
                        pe.wait_ge(y_kept, 2 * i + j)
                    for a in range(2):
                        mm = nc.tensor.matmul(ps_y[:, 256 * a:256 * a + 256], pr[:, par, 4, bass.ts(2 * j + a, P)], basis,
                                              start=True, stop=True)
                    mm.then_inc(y_summed, 1)

                tile_loop(pe, None, body)
                dft_cols(TILES - 1, 0, 0)
                dft_cols(TILES - 1, 0, 1)

            @block.vector
            def _(dve):
                def keep_h(i, par):
                    grp = 0 if isinstance(i, int) and i == 0 else 1
                    dve.wait_ge(x_turned, 2 * i + 1)
                    if not first(i):
                        dve.wait_ge(y_summed, 2 * i - 2)
                    for k in range(4):
                        g.dve.did(nc.vector.tensor_scalar(hT[:, par, k], ps_x[0][:, bass.ts(k, P)], g.mod[:, grp, 0, k:k + 1],
                                                          g.mod[:, grp, 1, k:k + 1], ALU.mult, ALU.add), hT_ready_dve)

                def body(i, par, half):
                    last = isinstance(i, int) and i == TILES - 1
                    for b in range(5):
                        if b == 3 and not last:
                            normed(nc, g, dve, i + 1, 1 - par, half + par)
                        if b == 4 and not last:
                            keep_h(i + 1, 1 - par)
                        dve.wait_ge(block_summed, 5 * i + b + 1)
                        if b == 0 and not first(i):
                            dve.wait_ge(qk_turned, 2 * i - 2)
                            dve.wait_ge(kvo_stored[par], 16 * half)
                        g.dve.did(nc.vector.tensor_tensor(pr[:, par, b], ps_p[(par + b) % 2][:], g.b_in_row[:, COLS[b]:COLS[b] + 512],
                                                          ALU.add), block_kept)
                    dve.wait_ge(gates_summed, i + 1)
                    g.dve.did(nc.vector.tensor_copy(g.gate_rows[:, bass.ts(i, P)], ps_g[:, 0:P]), gates_kept)

                keep_h(0, 0)
                g.dve.did(nc.vector.memset(w_gate[:], 0.0))
                dve.wait_ge(g.w_in_loaded, 16 * 4)
                g.dve.settle()
                for j, c in enumerate((0, 2, 1, 3)):
                    ins = nc.vector.tensor_copy(w_gate[:, :, 32 * j:32 * j + HEADS],
                                                g.w_in_sb[:, :, OFF_G + HEADS * c:OFF_G + HEADS * (c + 1)])
                    g.dve.did(ins, weights_set if j == 3 else None)
                dve.wait_ge(bg_loaded, 16 * 4)
                dve.wait_ge(g.b_in_loaded, 16)
                tile_loop(dve, g.dve, body, {"hT_ready_dve": 8, "block_kept": 10, "x_normed": 2, "gates_kept": 2})
                g.dve.settle()
                for j in range(4):
                    s = slice(32 * j, 32 * j + HEADS)
                    g.dve.did(nc.vector.tensor_scalar(g.gate_rows[s, :], g.gate_rows[s, :], b_gate[s, :], None, ALU.add))
                g.dve.settle()


def recurrence(nc, g):
    NR = 32 + HEADS
    KV = 4
    ctx = ExitStack()
    with ctx:
        def sb(name, shape):
            return ctx.enter_context(nc.sbuf_tensor(name, shape, F32))

        f_row = sb("f_row", [64, ROWS])
        b_row = sb("b_row", [64, ROWS])
        e_row = sb("e_row", [64, ROWS])
        t_row = sb("t_row", [64, ROWS])
        keep = sb("keep", [64, ROWS])
        wi_row = sb("wi_row", [64, ROWS])
        em_row = sb("em_row", [64, ROWS])
        b_last, e_last, m_last, wi_last = (sb(n, [64, TILES]) for n in ("b_last", "e_last", "m_last", "wi_last"))
        m_new, m_prev = sb("m_new", [64, TILES]), sb("m_prev", [64, TILES])
        m_init = sb("m_init", [64, 1])
        carry = sb("carry", [P, LANES, TILES])
        z_sb = sb("z_sb", [P, 2, 256])
        c_init = g.end_states
        n_init = sb("n_init", [LANES, HD])
        kv = sb("kv", [P, KV, 2, 2 * WIDTH])
        wv = sb("wv", [P, 2, LANES, VW])
        c_end = sb("c_end", [P, LANES, VW])
        c_out = c_init
        n_out = g.end_n
        bk = [ctx.enter_context(nc.psum_tensor(f"bk{i}", [P, 512], F32)) for i in range(8)]
        sem = g.sem
        init_loaded = sem("init_loaded")
        m_init_zeroed = sem("m_init_zeroed")
        kv_loaded = [[sem(f"kv_loaded{p}{d}") for d in range(2)] for p in range(KV)]
        f_abs_ready, soft_ready = sem("f_abs_ready"), sem("soft_ready")
        exponents_ready, weights_ready = sem("exponents_ready"), sem("weights_ready")
        z_summed, z_kept, f_summed, f_kept = sem("z_summed"), sem("z_kept"), sem("f_summed"), sem("f_kept")
        init_turned, init_kept = sem("init_turned"), sem("init_kept")
        cols_turned, cols_kept = sem("cols_turned"), sem("cols_kept")
        wi_last_ready, carry_spread, carry_kept = sem("wi_last_ready"), sem("carry_spread"), sem("carry_kept")
        wv_fwd, wv_bwd = sem("wv_fwd"), sem("wv_bwd")
        kv_summed, state_kept = sem("kv_summed"), sem("state_kept")
        end_turned, end_kept = sem("end_turned"), sem("end_kept")
        m_stored, states_stored = sem("m_stored"), g.states_stored
        m_new_ready = sem("m_new_ready")
        FWD, BWD = slice(0, 32), slice(32, 64)

        def chunks(x):
            return x.rearrange("p (n c) -> p n c", c=P)

        def lane_bank(par, r):
            return bk[(1, 5)[par] + r // 3], VW * (r % 3)

        with nc.Block() as block:
            @block.sync
            def _(sp):
                sp.dma_start(c_init[:], g.state_C.rearrange("(r v) k -> v r k", v=HD)).then_inc(init_loaded, 16)
                sp.dma_start(n_init[:], g.state_n).then_inc(init_loaded, 16)
                sp.wait_ge(m_init_zeroed, 1)
                with nc.allow_non_contiguous_dma("one stabiliser per partition"):
                    for d in range(2):
                        sp.dma_start(m_init[32 * d:32 * d + HEADS, :], g.state_m[HEADS * d:HEADS * d + HEADS, :]).then_inc(init_loaded, 16)

                def load(n):
                    if n >= KV:
                        sp.wait_ge(kv_summed, n - KV + 1)
                    for d in range(2 if n else 1):
                        tile = TILES - n if d else n
                        sp.dma_start(kv[:, n % KV, d], g.kvo[bass.ts(tile, P), 0:2 * WIDTH]).then_inc(kv_loaded[n % KV][d], 16)

                for n in range(KV):
                    load(n)
                sp.wait_ge(exponents_ready, 1)
                for d in range(2):
                    sp.dma_start(g.m_lanes.rearrange("t (r c) -> r t c", c=P)[HEADS * d:HEADS * d + HEADS],
                                 chunks(g.m_row[32 * d:32 * d + HEADS, :])).then_inc(m_stored, 16)
                sp.wait_ge(m_new_ready, 1)
                with nc.allow_non_contiguous_dma("one stabiliser per partition"):
                    for d in range(2):
                        sp.dma_start(g.new_m[HEADS * d:HEADS * d + HEADS, :], m_new[32 * d:32 * d + HEADS, 0:1]).then_inc(m_stored, 16)
                for n in range(KV, TILES - 1):
                    load(n)
                sp.wait_ge(end_kept, 3)
                sp.dma_start(g.new_C.rearrange("(r v) k -> v r k", v=HD), c_out[:]).then_inc(states_stored, 16)
                sp.dma_start(g.new_n, n_out[:]).then_inc(states_stored, 16)
                sp.wait_ge(m_stored, 64)

            @block.scalar
            def _(act):
                did, settle = g.act.did, g.act.settle
                act.wait_ge(f_abs_ready, 1)
                did(nc.scalar.activation(t_row[:], t_row[:], ACT.Exp, scale=-1.0))
                settle()
                did(nc.scalar.activation(t_row[:], t_row[:], ACT.Ln, bias=1.0), soft_ready)

                def keep_z(n):
                    act.wait_ge(z_summed, n + 1)
                    if n >= 2:
                        act.wait_ge(f_summed, n - 1)
                    did(nc.scalar.activation(z_sb[:, n % 2], bk[n % 2][:, 0:256], ACT.Copy), z_kept)

                def keep_f(n):
                    act.wait_ge(f_summed, n + 1)
                    grp, kcb = divmod(n, 8)
                    dst = g.fuT[:, grp, PROMPT:ROWS].rearrange("p (r c) -> p r c", c=GRID_W)[:, :, 8 * kcb:8 * kcb + 8]
                    did(nc.scalar.activation(dst, bk[2 + n % 2][:, 0:P].rearrange("p (r c) -> p r c", c=8), ACT.Copy,
                                             scale=(LATENT * HD) ** -0.5), f_kept)

                for n in range(33):
                    if n < 32:
                        keep_z(n)
                    if n >= 1:
                        keep_f(n - 1)
                    if n == 12:
                        act.wait_ge(exponents_ready, 3)
                        for row, scale in ((wi_row, -1.0), (em_row, -1.0), (t_row, 1.0)):
                            did(nc.scalar.activation(row[:], row[:], ACT.Exp, scale=scale), weights_ready)
                act.wait_ge(f_summed, 33)
                did(nc.scalar.activation(g.fuT[:, :, 0:P], bk[0][:].rearrange("p (a n) -> p a n", n=P), ACT.Copy,
                                         scale=(PROMPT * HD) ** -0.5), f_kept)
                for d in range(2):
                    act.wait_ge(end_turned, d + 1)
                    did(nc.scalar.activation(c_out[:, HEADS * d:HEADS * d + HEADS], bk[(4, 0)[d]][:].rearrange("p (r k) -> p r k", k=HD), ACT.Copy), end_kept)
                act.wait_ge(end_turned, 3)
                did(nc.scalar.activation(n_out[:], bk[2][0:LANES, 384:512], ACT.Copy), end_kept)
                settle()

            @block.gpsimd
            def _(pool):
                def weigh(n, par):
                    tile = TILES - n if n else 0
                    d = 1 if n else 0
                    pool.wait_ge(kv_loaded[n % KV][d], 16 * (n // KV + (1 if n % KV or n == 0 else 0)))
                    if n >= 2:
                        pool.wait_ge(kv_summed, n - 1)
                    nc.gpsimd.tensor_tensor(wv[:, par, HEADS:LANES, 0:HD], kv[:, n % KV, d, WIDTH:].rearrange("p (h v) -> p h v", v=HD),
                                            g.cols[:, 3, tile, HEADS:LANES, None].to_broadcast([P, HEADS, HD]), ALU.mult)
                    nc.gpsimd.tensor_copy(wv[:, par, HEADS:LANES, HD], g.cols[:, 3, tile, HEADS:LANES]).then_inc(wv_bwd, 1)

                pool.wait_ge(cols_kept, 8)
                for n in range(TILES - 1):
                    weigh(n, n % 2)

            @block.tensor
            def _(pe):
                pe.wait_ge(init_loaded, 64)
                for d in range(2):
                    for h in range(HEADS):
                        mm = nc.tensor.transpose(bk[4 + d][:, bass.ts(h, P)], c_init[:, HEADS * d + h], g.ident)
                mm = nc.tensor.transpose(bk[6][:, 0:LANES], n_init[:], g.ident[0:LANES, 0:LANES])
                mm.then_inc(init_turned, 1)

                def z_sum(n):
                    grp, kcb = divmod(n, 8)
                    if n >= 2:
                        pe.wait_ge(z_kept, n - 1)
                    for c, basis in ((0, g.dft_chan_r), (1, g.dft_chan_i)):
                        lhs = g.y[:, grp, c, bass.ts(kcb, P)]
                        mm = nc.tensor.matmul(bk[n % 2][:, 0:256], lhs, basis, start=(c == 0), stop=(c == 1))
                    mm.then_inc(z_summed, 1)

                def f_sum(n):
                    pe.wait_ge(z_kept, n + 1)
                    if n >= 2:
                        pe.wait_ge(f_kept, n - 1)
                    for c, basis in ((0, g.dft_row_c), (1, g.dft_row_s)):
                        mm = nc.tensor.matmul(bk[2 + n % 2][:, 0:P], z_sb[:, n % 2, bass.ts(c, P)], basis, start=(c == 0), stop=(c == 1))
                    mm.then_inc(f_summed, 1)

                for n in range(33):
                    if n < 32:
                        z_sum(n)
                    if n >= 1:
                        f_sum(n - 1)
                pe.wait_ge(z_kept, 32)
                for grp in range(4):
                    for c, basis in ((0, g.dft_chan_r), (1, g.dft_chan_i)):
                        mm = nc.tensor.matmul(bk[0][:, bass.ts(grp, P)], basis[:, 0:P], g.y_prompt[:, grp, c], start=(c == 0), stop=(c == 1))
                mm.then_inc(f_summed, 1)
                pe.wait_ge(weights_ready, 3)
                pe.wait_ge(init_kept, 4)
                for q, row in enumerate((e_row, wi_row, em_row, t_row)):
                    for i in range(TILES):
                        mm = nc.tensor.transpose(bk[4 + q][:, NR * i:NR * i + NR], row[0:NR, bass.ts(i, P)], g.ident[0:NR, 0:NR])
                    mm.then_inc(cols_turned, 1)
                pe.wait_ge(wi_last_ready, 1)
                pe.wait_ge(f_kept, 32)
                for r in range(LANES):
                    mm = nc.tensor.matmul(bk[2][:, TILES * r:TILES * r + TILES], g.pick_lane[0:64, bass.ts(r, P)], wi_last[:], start=True, stop=True)
                mm.then_inc(carry_spread, 1)
                pe.wait_ge(carry_kept, 1)
                pe.wait_ge(cols_kept, 8)
                for n in range(TILES - 1):
                    par = n % 2
                    pe.wait_ge(wv_fwd, n + 1)
                    pe.wait_ge(wv_bwd, n + 1)
                    if n >= 2:
                        pe.wait_ge(state_kept, LANES * (n - 1))
                    for r in range(LANES):
                        bank, at = lane_bank(par, r)
                        d = 1 if n and r >= HEADS else 0
                        mm = nc.tensor.matmul(bank[:, at:at + VW], kv[:, n % KV, d, bass.ts(r % HEADS, P)], wv[:, par, r], start=True, stop=True)
                    mm.then_inc(kv_summed, 1)
                pe.wait_ge(f_kept, 33)
                pe.wait_ge(state_kept, LANES * 8)
                for d in range(2):
                    for h in range(HEADS):
                        mm = nc.tensor.transpose(bk[(4, 0)[d]][:, bass.ts(h, P)], c_end[:, HEADS * d + h, 0:HD], g.ident)
                    mm.then_inc(end_turned, 1)
                nc.tensor.transpose(bk[2][0:LANES, 384:512], c_end[:, :, HD], g.ident).then_inc(end_turned, 1)

            @block.vector
            def _(dve):
                did, settle = g.dve.did, g.dve.settle
                TT, TS, STT = nc.vector.tensor_tensor, nc.vector.tensor_scalar, nc.vector.scalar_tensor_tensor
                did(nc.vector.memset(m_init[:], 0.0), m_init_zeroed)
                did(nc.vector.tensor_copy(f_row[:], g.gate_rows[64:128, :]))
                settle()
                did(STT(t_row[:], f_row[:], -1.0, f_row[:], ALU.mult, ALU.max), f_abs_ready)
                did(nc.vector.memset(keep[:], 1.0))
                did(nc.vector.memset(m_prev[:], 0.0))
                did(nc.vector.memset(g.states[:, 0], 0.0))
                did(nc.vector.memset(g.eps[:], EPS))
                settle()
                did(nc.vector.memset(chunks(keep[FWD, :])[:, :, 0], 0.0))
                did(nc.vector.memset(chunks(keep[BWD, :])[:, :, P - 1], 0.0))
                dve.wait_ge(init_turned, 1)
                for d, slot in ((0, 1), (1, TILES - 1)):
                    lanes = slice(HEADS * d, HEADS * d + HEADS)
                    did(nc.vector.tensor_copy(g.states[:, slot, lanes, 0:HD], bk[4 + d][:].rearrange("p (r k) -> p r k", k=HD)), init_kept)
                    did(nc.vector.tensor_copy(g.states[:, slot, lanes, HD], bk[6][:, lanes]), init_kept)
                dve.wait_ge(soft_ready, 1)
                did(STT(f_row[:], f_row[:], 0.0, t_row[:], ALU.min, ALU.subtract))
                settle()
                did(nc.vector.tensor_tensor_scan(b_row[FWD, :], keep[FWD, :], f_row[FWD, :], 0.0, ALU.mult, ALU.add))
                did(nc.vector.tensor_tensor_scan(b_row[BWD, ::-1], keep[BWD, ::-1], f_row[BWD, ::-1], 0.0, ALU.mult, ALU.add))
                settle()
                did(TT(e_row[:], g.gate_rows[0:64, :], b_row[:], ALU.subtract))
                did(TS(keep[:], keep[:], -1.0, HUGE, ALU.add, ALU.mult))
                settle()
                did(nc.vector.tensor_tensor_scan(g.m_row[FWD, :], keep[FWD, :], e_row[FWD, :], 0.0, ALU.add, ALU.max))
                did(nc.vector.tensor_tensor_scan(g.m_row[BWD, ::-1], keep[BWD, ::-1], e_row[BWD, ::-1], 0.0, ALU.add, ALU.max))
                settle()
                for rows, at in ((FWD, P - 1), (BWD, 0)):
                    did(nc.vector.tensor_copy(b_last[rows, :], chunks(b_row[rows, :])[:, :, at]))
                    did(nc.vector.tensor_copy(e_last[rows, :], chunks(g.m_row[rows, :])[:, :, at]))
                dve.wait_ge(init_loaded, 64)
                settle()
                did(TS(m_new[:, 0:1], e_last[:, 0:1], 0.0, b_last[:, 0:1], ALU.max, ALU.add), m_new_ready)
                did(nc.vector.tensor_tensor_scan(m_new[FWD, 1:], e_last[FWD, 1:], b_last[FWD, 1:], m_init[FWD, :], ALU.max, ALU.add))
                did(nc.vector.tensor_tensor_scan(m_new[BWD, 1:][:, ::-1], e_last[BWD, 1:][:, ::-1], b_last[BWD, 1:][:, ::-1],
                                                 m_init[BWD, :], ALU.max, ALU.add))
                did(nc.vector.tensor_copy(m_prev[FWD, 1:2], m_init[FWD, :]))
                did(nc.vector.tensor_copy(m_prev[BWD, TILES - 1:TILES], m_init[BWD, :]))
                settle()
                did(nc.vector.tensor_copy(m_prev[FWD, 2:], m_new[FWD, 1:TILES - 1]))
                did(nc.vector.tensor_copy(m_prev[BWD, 1:TILES - 1], m_new[BWD, 2:]))
                settle()
                spread = [64, TILES, P]
                did(TT(chunks(g.m_row), chunks(g.m_row), m_prev[:, :, None].to_broadcast(spread), ALU.max))
                settle()
                did(TT(chunks(wi_row[:]), chunks(g.m_row), m_prev[:, :, None].to_broadcast(spread), ALU.subtract), exponents_ready)
                did(TT(em_row[:], b_row[:], g.m_row[:], ALU.add), exponents_ready)
                for rows, at in ((FWD, P - 1), (BWD, 0)):
                    did(nc.vector.tensor_copy(m_last[rows, :], chunks(g.m_row[rows, :])[:, :, at]))
                settle()
                did(TT(chunks(t_row[:]), chunks(e_row[:]), m_last[:, :, None].to_broadcast(spread), ALU.subtract), exponents_ready)
                dve.wait_ge(weights_ready, 1)
                for rows, at in ((FWD, P - 1), (BWD, 0)):
                    did(nc.vector.tensor_copy(wi_last[rows, :], chunks(wi_row[rows, :])[:, :, at]), wi_last_ready if at == 0 else None)
                for q in range(4):
                    dve.wait_ge(cols_turned, q + 1)
                    src = bk[4 + q][:, 0:NR * TILES].rearrange("p (n c) -> p n c", c=NR)
                    for d in range(2):
                        did(TS(g.cols[:, q, :, HEADS * d:HEADS * d + HEADS], src[:, :, 32 * d:32 * d + HEADS],
                               K_SCALE if q == 3 else 1.0, None, ALU.mult), cols_kept)
                dve.wait_ge(carry_spread, 1)
                did(nc.vector.tensor_copy(carry[:], bk[2][:, 0:LANES * TILES].rearrange("p (r n) -> p r n", n=TILES)), carry_kept)
                settle()

                def weigh(n, par):
                    dve.wait_ge(kv_loaded[n % KV][0], 16 * (n // KV + 1))
                    if n >= 2:
                        dve.wait_ge(kv_summed, n - 1)
                    did(TT(wv[:, par, 0:HEADS, 0:HD], kv[:, n % KV, 0, WIDTH:].rearrange("p (h v) -> p h v", v=HD),
                           g.cols[:, 3, n, 0:HEADS, None].to_broadcast([P, HEADS, HD]), ALU.mult))
                    did(nc.vector.tensor_copy(wv[:, par, 0:HEADS, HD], g.cols[:, 3, n, 0:HEADS]), wv_fwd)

                weigh(0, 0)
                for n in range(TILES - 1):
                    par = n % 2
                    if n + 1 < TILES - 1:
                        weigh(n + 1, 1 - par)
                    dve.wait_ge(kv_summed, n + 1)
                    if n:
                        settle()
                    for r in range(LANES):
                        bank, at = lane_bank(par, r)
                        src = bank[:, at:at + VW]
                        if n == 0:
                            did(nc.vector.tensor_copy(c_end[:, r], src), state_kept)
                        else:
                            frm, to = (n, n + 1) if r < HEADS else (TILES - n, TILES - 1 - n)
                            did(STT(g.states[:, to, r], g.states[:, frm, r], carry[:, r, frm:frm + 1], src, ALU.mult, ALU.add), state_kept)
                settle()


def below(i, n):
    return isinstance(i, int) and i < n


def mixing(nc, g):
    ctx = ExitStack()
    with ctx:
        def sb(name, shape):
            return ctx.enter_context(nc.sbuf_tensor(name, shape, F32))

        va = sb("va", [P, 2, HEADS, VW])
        o_in = sb("o_in", [P, 2, WIDTH])
        qk = sb("qk", [P, 2, 2 * HEADS, P])
        m_in = sb("m_in", [P, 2, LANES * P])
        x_in = sb("x_in", [P, 2, D])
        wgt = sb("wgt", [P, 2, HEADS, P])
        num = sb("num", [P, 2, HEADS, VW])
        den = sb("den", [P, LANES])
        hm, hm2 = sb("hm", [P, HEADS, HD]), sb("hm2", [P, HEADS, HD])
        hms = sb("hms", [P, HEADS])
        og, gain = sb("og", [P, WIDTH]), sb("gain", [P, WIDTH])
        head_g = sb("head_g_row", [P, WIDTH])
        mixT = sb("mixT", [P, 2, DT, P])
        x2 = sb("x2", [P, 2, D])
        xn2 = sb("xn2", [P, D])
        squares = ctx.enter_context(nc.sbuf_tensor("squares2", [P, 512], mybir.dt.bfloat16))
        ss = sb("ss", [P, 4])
        h2T = sb("h2T", [P, DT, P])
        router = sb("router", [P, DT, E])
        logits = sb("logits", [P, P])
        aff = sb("aff", [P, E])
        soft = sb("soft", [P, 4])

        def bank(name):
            return ctx.enter_context(nc.psum_tensor(name, [P, 512], F32))

        b_s, b_m = bank("b_s"), bank("b_m")
        b_n = [bank(f"b_n{i}") for i in range(2)]
        b_i = [bank(f"b_i{i}") for i in range(2)]
        b_z = [bank(f"b_z{i}") for i in range(2)]
        ps_logits, ps_affT = b_z[1][0:E, 0:P], b_s[0:E, 0:P]
        sem = g.sem
        pair = lambda name: [sem(f"{name}{i}") for i in range(2)]
        qk_loaded, v_loaded, o_loaded, xr_loaded = pair("qk_loaded"), pair("v_loaded"), pair("o_loaded"), pair("xr_loaded")
        stream_stored, m_loaded = pair("stream_stored"), pair("m_loaded")
        normed_stored, consts_loaded, ones_set = sem("normed_stored"), sem("consts_loaded"), sem("ones_set")
        (scores_summed, x_ready, w_ready, p_ready, inter_summed, inter_kept, intra_summed, comb_done,
         out_summed, out_kept, x2_ready, sq_summed, rms2_ready, xn2_ready, x2_turned, h2T_dve, h2T_act,
         logits_summed, logits_kept, logits_turned, negmax_ready, soft_exped, aff_ready, aff_turned, aff_kept,
         hm_ready, hm_turned, mix_act, mix_pool, og_exped, og_ready, gain_ready, hms_ready, rh_ready, ss_steps) = (
            sem(n) for n in (
                "scores_summed", "x_ready", "w_ready", "p_ready", "inter_summed", "inter_kept", "intra_summed",
                "comb_done", "out_summed", "out_kept", "x2_ready", "sq_summed", "rms2_ready", "xn2_ready", "x2_turned",
                "h2T_dve", "h2T_act", "logits_summed", "logits_kept", "logits_turned", "negmax_ready", "soft_exped",
                "aff_ready", "aff_turned", "aff_kept", "hm_ready", "hm_turned", "mix_act", "mix_pool", "og_exped",
                "og_ready", "gain_ready", "hms_ready", "rh_ready", "ss_steps"))

        def group(t):
            return 0 if below(t, 1) else 1

        def on(i, lag):
            return not below(i, lag) and not (isinstance(i, int) and i - lag >= TILES)

        def turns(engine, steps, turn, per=None):
            for i in range(5):
                turn(i, i % 2, i // 2)
            with (engine.Fori(0, 2) if steps is None else steps.loop(engine, 2, per)) as j:
                turn(j * 2 + 5, 1, j + 2)
                turn(j * 2 + 6, 0, j + 3)
            for i in range(9, TILES + 4):
                turn(i, i % 2, i // 2)

        with nc.Block() as block:
            @block.sync
            def _(sp):
                def load(i, par, fresh):
                    if not fresh:
                        sp.wait_ge(inter_summed, 2 * i - 2)
                        sp.wait_ge(intra_summed, 2 * i - 2)
                        sp.wait_ge(og_exped, i - 1)
                    sp.dma_start(qk[:, par].rearrange("p h n -> p (h n)"), g.qkT[bass.ts(i, P), :]).then_inc(qk_loaded[par], 16)
                    sp.dma_start(m_in[:, par], g.m_lanes[bass.ds(i, 1), :].to_broadcast([P, LANES * P])).then_inc(m_loaded[par], 16)
                    sp.dma_start(va[:, par, :, 0:HD], g.kvo[bass.ts(i, P), WIDTH:2 * WIDTH].rearrange("p (h v) -> p h v", v=HD)).then_inc(v_loaded[par], 16)
                    sp.dma_start(o_in[:, par], g.kvo[bass.ts(i, P), 2 * WIDTH:3 * WIDTH]).then_inc(o_loaded[par], 16)

                def load_x(i, par):
                    sp.dma_start(x_in[:, par], g.x_rows(i)).then_inc(xr_loaded[par], 16)

                load(0, 0, True)
                load(1, 1, True)
                sp.dma_start(head_g[:], g.head_g.to_broadcast([P, WIDTH])).then_inc(consts_loaded, 16)
                sp.dma_start(router[:], g.router_w.rearrange("(k p) e -> p k e", p=P)).then_inc(consts_loaded, 16)
                load_x(0, 0)
                load_x(1, 1)
                for n in range(DT // 2):
                    sp.dma_start(g.w_out_sb[:, 2 * n:2 * n + 2], g.w_out_src[:, 2 * n:2 * n + 2]).then_inc(g.w_out_loaded, 16)

                def turn(i, par, half):
                    if not below(i, 1) and not (isinstance(i, int) and i >= TILES - 1):
                        load(i + 1, 1 - par, False)
                    if on(i, 3):
                        sp.wait_ge(xn2_ready, i - 2)
                        sp.dma_start(g.normed[bass.ts(i - 3, P), :], xn2[:]).then_inc(normed_stored, 16)
                    if on(i, 2):
                        sp.wait_ge(x2_ready, 2 * i - 2)
                        sp.dma_start(g.stream[bass.ts(i - 2, P), :], x2[:, par]).then_inc(stream_stored[par], 16)
                        if on(i, 0):
                            load_x(i, par)

                for i in range(4):
                    turn(i, i % 2, i // 2)
                with sp.Fori(2, 4) as j:
                    turn(j * 2, 0, j)
                    turn(j * 2 + 1, 1, j)
                for i in range(8, TILES + 3):
                    turn(i, i % 2, i // 2)
                for par, n in ((0, 5), (1, 4)):
                    sp.wait_ge(stream_stored[par], 16 * n)
                sp.wait_ge(normed_stored, 16 * TILES)
                sp.wait_ge(g.states_stored, 32)

            @block.gpsimd
            def _(pool):
                pool.wait_ge(consts_loaded, 32)

                def turn(i, par, half):
                    T = i - 2
                    if on(i, 1):
                        pool.wait_ge(hms_ready, i)
                        nc.gpsimd.tensor_tensor(hms[:], hms[:], g.minus_half[:], ALU.pow).then_inc(rh_ready, 1)
                    if on(i, 0):
                        pool.wait_ge(og_ready, i + 1)
                        if not below(i, 1):
                            pool.wait_ge(hm_ready, i)
                        nc.gpsimd.tensor_tensor(gain[:], og[:], head_g[:], ALU.mult).then_inc(gain_ready, 1)
                    if on(i, 2):
                        pool.wait_ge(sq_summed, 2 * i - 2)
                        if not below(i, 3):
                            pool.wait_ge(xn2_ready, i - 2)
                        nc.gpsimd.tensor_tensor(ss[:, 2:3], ss[:, 0:1], ss[:, 1:2], ALU.add).then_inc(ss_steps, 1)
                        pool.wait_ge(ss_steps, T * 2 + 1)
                        nc.gpsimd.tensor_tensor(ss[:, 2:3], ss[:, 2:3], g.eps[:], ALU.add).then_inc(ss_steps, 1)
                        pool.wait_ge(ss_steps, T * 2 + 2)
                        nc.gpsimd.tensor_tensor(ss[:, 3:4], ss[:, 2:3], g.minus_half[:, 0:1], ALU.pow).then_inc(rms2_ready, 1)
                    if on(i, 0):
                        if not below(i, 2):
                            pool.wait_ge(out_summed, 2 * i - 2)
                        nc.gpsimd.tensor_copy(mixT[:, par, HEADS:DT], g.fuT[:, :, bass.ts(i, P)]).then_inc(mix_pool, 1)

                turns(pool, None, turn)

            @block.scalar
            def _(act):
                did = g.act.did

                def front(i, par, half):
                    act.wait_ge(o_loaded[par], 16 * (half + 1))
                    if not below(i, 1):
                        act.wait_ge(gain_ready, i)
                    did(nc.scalar.activation(og[:], o_in[:, par], ACT.Exp, scale=-1.0), og_exped)

                def weigh(i, d):
                    act.wait_ge(x_ready, 2 * i + (d + 1))
                    did(nc.scalar.activation(wgt[:, d], wgt[:, d], ACT.Exp, scale=-1.0), w_ready)

                def inter(i, d):
                    act.wait_ge(inter_summed, 2 * i + (d + 1))
                    if not below(i, 1):
                        act.wait_ge(hm_ready, i)
                    for h in range(HEADS):
                        did(nc.scalar.activation(num[:, d, h], b_i[h // 2][:, VW * (h % 2):VW * (h % 2) + VW], ACT.Copy,
                                                 scale=g.cols[:, 1, i, HEADS * d + h:HEADS * d + h + 1] if isinstance(i, int)
                                                 else g.cols[:, 1, bass.ds(i, 1), HEADS * d + h]), inter_kept if h == HEADS - 1 else None)

                def square(i, par, h):
                    act.wait_ge(x2_ready, 2 * i + (h - 3))
                    if not below(i, 3):
                        act.wait_ge(rms2_ready, i - 2)
                    g.act.settle()
                    did(nc.scalar.activation(squares[:], x2[:, par, bass.ts(h, 512)], ACT.Square, scale=D ** -0.5, accum_out=ss[:, h:h + 1]), sq_summed)

                def turn(i, par, half):
                    if on(i, 0):
                        front(i, par, half)
                        weigh(i, 0)
                    if on(i, 4):
                        act.wait_ge(negmax_ready, i - 3)
                        if not below(i, 5):
                            act.wait_ge(aff_turned, i - 4)
                        did(nc.scalar.activation(aff[:], b_z[1][:, 0:E], ACT.Exp, bias=soft[:, 0:1], accum_out=soft[:, 1:2]), soft_exped)
                    if on(i, 0):
                        inter(i, 0)
                    if on(i, 2):
                        square(i, par, 0)
                    if on(i, 0):
                        weigh(i, 1)
                        inter(i, 1)
                    if on(i, 3):
                        act.wait_ge(x2_turned, i - 2)
                        if on(i, 4):
                            act.wait_ge(logits_summed, i - 3)
                        for k in range(4, DT):
                            did(nc.scalar.activation(h2T[:, k], b_z[1][:, bass.ts(k - 4, P)], ACT.Identity,
                                                     scale=g.mod[:, group(i - 3), 2, k:k + 1], bias=g.mod[:, group(i - 3), 3, k:k + 1]),
                                h2T_act if k == DT - 1 else None)
                    if on(i, 1):
                        act.wait_ge(hm_turned, i)
                        if not below(i, 3):
                            act.wait_ge(out_summed, 2 * i - 4)
                        did(nc.scalar.activation(mixT[:, 1 - par, 0:HEADS], b_m[:].rearrange("p (h n) -> p h n", n=P), ACT.Copy), mix_act)
                    if on(i, 2):
                        square(i, par, 1)

                turns(act, g.act, turn, {"og_exped": 2, "w_ready": 4, "inter_kept": 4, "act_steps": 18, "sq_summed": 4,
                                         "soft_exped": 2, "h2T_act": 2, "mix_act": 2})

            @block.tensor
            def _(pe):
                def score(i, par, half):
                    pe.wait_ge(qk_loaded[par], 16 * (half + 1))
                    if not below(i, 1):
                        pe.wait_ge(p_ready, 2 * i)
                    if not below(i, 5):
                        pe.wait_ge(aff_kept, i - 4)
                    for h in range(HEADS):
                        mm = nc.tensor.matmul(b_s[:, bass.ts(h, P)], qk[:, par, HEADS + h], qk[:, par, h], start=True, stop=True)
                    mm.then_inc(scores_summed, 1)

                def inter(i, par, d):
                    if not below(2 * i + d, 1):
                        pe.wait_ge(inter_kept, 2 * i + d)
                    for h in range(HEADS):
                        mm = nc.tensor.matmul(b_i[h // 2][:, VW * (h % 2):VW * (h % 2) + VW], qk[:, par, h],
                                              g.states[:, i, HEADS * d + h] if isinstance(i, int) else
                                              g.states[:, bass.ds(i, 1), HEADS * d + h].rearrange("p a v -> p (a v)"), start=True, stop=True)
                    mm.then_inc(inter_summed, 1)

                def intra(i, par, half, d):
                    pe.wait_ge(p_ready, 2 * i + (d + 1))
                    pe.wait_ge(v_loaded[par], 16 * (half + 1))
                    if not below(2 * i + d, 1):
                        pe.wait_ge(comb_done, 2 * i + d)
                    for h in range(HEADS):
                        mm = nc.tensor.matmul(b_n[h // 2][:, VW * (h % 2):VW * (h % 2) + VW], wgt[:, d, h], va[:, par, h], start=True, stop=True)
                    mm.then_inc(intra_summed, 1)

                def project(i, par, h):
                    pe.wait_ge(mix_act, i - 1)
                    pe.wait_ge(mix_pool, i - 1)
                    if not below(i, 3):
                        pe.wait_ge(out_kept, 2 * i + (h - 5))
                    for k in range(DT):
                        mm = nc.tensor.matmul(b_z[h][:], mixT[:, par, k], g.w_out_sb[:, k, bass.ts(h, 512)], start=(k == 0), stop=(k == DT - 1))
                    mm.then_inc(out_summed, 1)

                def turn_rows(i):
                    pe.wait_ge(xn2_ready, i - 2)
                    if on(i, 2):
                        pe.wait_ge(out_kept, 2 * i - 2)
                    elif on(i, 4):
                        pe.wait_ge(soft_exped, i - 3)
                    for k in range(DT):
                        mm = nc.tensor.transpose(b_z[k // 4][:, bass.ts(k % 4, P)], xn2[:, bass.ts(k, P)], g.ident)
                    mm.then_inc(x2_turned, 1)

                def route(i):
                    pe.wait_ge(h2T_dve, i - 3)
                    pe.wait_ge(h2T_act, i - 3)
                    for k in range(DT):
                        mm = nc.tensor.matmul(ps_logits, router[:, k], h2T[:, k], start=(k == 0), stop=(k == DT - 1))
                    mm.then_inc(logits_summed, 1)

                pe.wait_ge(ones_set, 1)

                def turn(i, par, half):
                    if on(i, 0):
                        score(i, par, half)
                        inter(i, par, 0)
                    if on(i, 4):
                        route(i)
                    if on(i, 2):
                        if below(i, 3):
                            pe.wait_ge(g.w_out_loaded, 16 * (DT // 2))
                            pe.wait_ge(consts_loaded, 32)
                        project(i, par, 0)
                    if on(i, 4):
                        pe.wait_ge(logits_kept, i - 3)
                        nc.tensor.transpose(b_z[1][:, 0:P], logits[:], g.ident).then_inc(logits_turned, 1)
                    if on(i, 0):
                        intra(i, par, half, 0)
                    if on(i, 2):
                        if on(i, 4):
                            pe.wait_ge(soft_exped, i - 3)
                        project(i, par, 1)
                    if on(i, 4):
                        pe.wait_ge(aff_ready, i - 3)
                        if on(i, 0):
                            pe.wait_ge(p_ready, 2 * i + 2)
                        else:
                            pe.wait_ge(aff_kept, i - 4)
                        nc.tensor.transpose(ps_affT, aff[:], g.ident).then_inc(aff_turned, 1)
                    if on(i, 0):
                        inter(i, par, 1)
                        intra(i, par, half, 1)
                    if on(i, 3):
                        turn_rows(i)
                    if on(i, 1):
                        pe.wait_ge(hm_ready, i)
                        if not below(i, 2):
                            pe.wait_ge(mix_act, i - 1)
                        for h in range(HEADS):
                            mm = nc.tensor.transpose(b_m[:, bass.ts(h, P)], hm[:, h], g.ident)
                        mm.then_inc(hm_turned, 1)

                turns(pe, None, turn)

            @block.vector
            def _(dve):
                did, settle = g.dve.did, g.dve.settle
                TT, TS, STT = nc.vector.tensor_tensor, nc.vector.tensor_scalar, nc.vector.scalar_tensor_tensor
                COPY = nc.vector.tensor_copy
                did(nc.vector.memset(logits[:], 0.0))
                did(nc.vector.memset(g.aff_rows[:], 0.0))
                did(nc.vector.memset(va[:, :, :, HD], 1.0), ones_set)
                settle()

                def exponents(i, par, half, d):
                    dve.wait_ge(m_loaded[par], 16 * (half + 1))
                    if not below(i, 1):
                        dve.wait_ge(intra_summed, 2 * i + (d - 1))
                    for h in range(HEADS):
                        e = g.cols[:, 0, i, HEADS * d + h:HEADS * d + h + 1] if isinstance(i, int) else g.cols[:, 0, bass.ds(i, 1), HEADS * d + h]
                        did(STT(wgt[:, d, h], m_in[:, par, bass.ts(HEADS * d + h, P)], e, g.masks[:, bass.ts(d, P)], ALU.subtract, ALU.max),
                            x_ready if h == HEADS - 1 else None)

                def weighted(i, d):
                    dve.wait_ge(w_ready, 2 * i + (d + 1))
                    dve.wait_ge(scores_summed, i + 1)
                    did(TT(wgt[:, d], wgt[:, d], b_s[:].rearrange("p (h n) -> p h n", n=P), ALU.mult), p_ready)

                def residual(i, par, half, h):
                    grp = group(i - 2)
                    cols = bass.ts(h, 512)
                    dve.wait_ge(out_summed, 2 * i + (h - 3))
                    if h == 0:
                        dve.wait_ge(xr_loaded[par], 16 * half)
                        if not below(i, 4):
                            dve.wait_ge(stream_stored[par], 16 * half - 16)
                    did(TT(x2[:, par, cols], b_z[h][:], g.gate1[:, grp, cols], ALU.mult), out_kept)
                    settle()
                    did(TT(x2[:, par, cols], x2[:, par, cols], x_in[:, par, cols], ALU.add), x2_ready)

                def combine(i, d):
                    dve.wait_ge(inter_kept, 2 * i + (d + 1))
                    dve.wait_ge(intra_summed, 2 * i + (d + 1))
                    for b in range(2):
                        did(TT(num[:, d, 2 * b:2 * b + 2], num[:, d, 2 * b:2 * b + 2], b_n[b][:, 0:2 * VW].rearrange("p (h v) -> p h v", v=VW),
                               ALU.add), comb_done if b else None)

                def outputs(i):
                    settle()
                    nums = num[:].rearrange("p d h v -> p (d h) v")
                    did(STT(den[:], nums[:, :, HD], -1.0, nums[:, :, HD], ALU.mult, ALU.max))
                    settle()
                    em = g.cols[:, 2, i - 1] if isinstance(i, int) else g.cols[:, 2, bass.ds(i - 1, 1)].rearrange("p a r -> p (a r)")
                    did(TT(den[:], den[:], em, ALU.max))
                    settle()
                    did(nc.vector.reciprocal(den[:], den[:]))
                    settle()
                    if not below(i, 2):
                        dve.wait_ge(hm_turned, i - 1)
                    wide = [P, HEADS, HD]
                    did(TT(hm[:], num[:, 0, :, 0:HD], den[:, 0:HEADS, None].to_broadcast(wide), ALU.mult))
                    did(TT(hm2[:], num[:, 1, :, 0:HD], den[:, HEADS:, None].to_broadcast(wide), ALU.mult))
                    settle()
                    did(TT(hm[:], hm[:], hm2[:], ALU.add))
                    settle()
                    did(TT(hm2[:], hm[:], hm[:], ALU.mult))
                    settle()
                    did(nc.vector.tensor_reduce(hms[:], hm2[:], AX.X, ALU.add))
                    settle()
                    did(TS(hms[:], hms[:], 1.0 / HD, EPS, ALU.mult, ALU.add), hms_ready)
                    dve.wait_ge(gain_ready, i)
                    did(TT(hm[:], hm[:], gain[:].rearrange("p (h v) -> p h v", v=HD), ALU.mult))
                    settle()
                    dve.wait_ge(rh_ready, i)
                    did(TT(hm[:], hm[:], hms[:, :, None].to_broadcast(wide), ALU.mult), hm_ready)

                def turn(i, par, half):
                    if on(i, 0):
                        exponents(i, par, half, 0)
                        weighted(i, 0)
                    if on(i, 4):
                        dve.wait_ge(logits_summed, i - 3)
                        if not below(i, 5):
                            dve.wait_ge(logits_turned, i - 4)
                        did(COPY(logits[0:E, :], ps_logits), logits_kept)
                    if on(i, 1):
                        outputs(i)
                    if on(i, 4):
                        dve.wait_ge(logits_turned, i - 3)
                        did(nc.vector.tensor_reduce(soft[:, 0:1], b_z[1][:, 0:E], AX.X, ALU.max, negate=True), negmax_ready)
                    if on(i, 3):
                        dve.wait_ge(rms2_ready, i - 2)
                        if not below(i, 4):
                            dve.wait_ge(x2_turned, i - 3)
                            dve.wait_ge(normed_stored, 16 * i - 48)
                        did(TS(xn2[:], x2[:, 1 - par], ss[:, 3:4], None, ALU.mult), xn2_ready)
                    if on(i, 2):
                        residual(i, par, half, 0)
                    if on(i, 0):
                        combine(i, 0)
                        exponents(i, par, half, 1)
                    if on(i, 4):
                        dve.wait_ge(soft_exped, i - 3)
                        did(nc.vector.reciprocal(soft[:, 2:3], soft[:, 1:2]))
                        settle()
                        did(TS(aff[:], aff[:], soft[:, 2:3], None, ALU.mult), aff_ready)
                    if on(i, 0):
                        dve.wait_ge(og_exped, i + 1)
                        did(TS(og[:], og[:], 1.0, None, ALU.add))
                        weighted(i, 1)
                        settle()
                        did(nc.vector.reciprocal(og[:], og[:]), og_ready)
                    if on(i, 2):
                        residual(i, par, half, 1)
                    if on(i, 4):
                        dve.wait_ge(aff_turned, i - 3)
                        if isinstance(i, int) and i - 4 > TILES // 2:
                            dst = g.aff_rows[SECOND:HALVES, bass.ts(i - 4 - TILES // 2, P)]
                        else:
                            dst = g.aff_rows[0:E, bass.ts(i - 4, P)]
                        did(COPY(dst, ps_affT), aff_kept)
                    if on(i, 3):
                        dve.wait_ge(x2_turned, i - 2)
                        for k in range(4):
                            did(TS(h2T[:, k], b_z[0][:, bass.ts(k, P)], g.mod[:, group(i - 3), 2, k:k + 1], g.mod[:, group(i - 3), 3, k:k + 1],
                                   ALU.mult, ALU.add), h2T_dve if k == 3 else None)
                    if on(i, 0):
                        combine(i, 1)

                turns(dve, g.dve, turn, {
                    "dve_steps": 44, "x_ready": 4, "p_ready": 4, "og_ready": 2, "negmax_ready": 2, "out_kept": 4, "x2_ready": 4,
                    "comb_done": 4, "aff_ready": 2, "xn2_ready": 2, "aff_kept": 2, "h2T_dve": 2, "hms_ready": 2, "hm_ready": 2,
                    "logits_kept": 2})
                settle()


def routing(nc, g):
    ctx = ExitStack()
    with ctx:
        def sb(name, shape, dt=F32):
            return ctx.enter_context(nc.sbuf_tensor(name, shape, dt))

        top, at, at_f = sb("top", [HALVES, CAP_L]), sb("at", [HALVES, CAP_L], U32), sb("at_f", [HALVES, CAP_L])
        top_b, at_b = sb("top_b", [E, CAP_L]), sb("at_b", [E, CAP_L])
        top_p, at_p, at_pf = sb("top_p", [E, CAP_P]), sb("at_p", [E, CAP_P], U32), sb("at_pf", [E, CAP_P])
        spare = sb("spare", [HALVES, LATENT // 2])
        prompt_slots = sb("prompt_slots", [CAP_P, 2 * E])
        first_wins, gap = sb("first_wins", [P, E]), sb("gap", [P, E])
        gate_b, row_b, row_f = sb("gate_b", [P, E]), sb("row_b", [P, E]), sb("row_f", [P, E])
        ps = [ctx.enter_context(nc.psum_tensor(f"ps_route{i}", [P, 512], F32)) for i in range(2)]
        picked, slots_turned = g.sem("picked"), g.sem("slots_turned")

        with nc.Block() as block:
            @block.sync
            def _(sp):
                for p in range(g.RING // 2):
                    g.load_pair(sp, 0, p)

            @block.tensor
            def _(pe):
                ident = g.ident[0:E, 0:E]
                pe.wait_ge(picked, 1)
                nc.tensor.transpose(ps[1][0:CAP_P, 0:E], top_p[:], ident)
                nc.tensor.transpose(ps[1][0:CAP_P, E:2 * E], at_pf[:], ident).then_inc(slots_turned, 1)
                pe.wait_ge(picked, 2)
                nc.tensor.matmul(ps[1][:, bass.ts(1, 2 * E)], g.spread_slots[0:CAP_P, :], prompt_slots[:], start=True, stop=True).then_inc(slots_turned, 1)
                pe.wait_ge(picked, 4)
                for n, src in enumerate((top[0:E, :], at_f[0:E, :], top_b[:], at_b[:])):
                    mm = nc.tensor.transpose(ps[0][:, bass.ts(n, E)], src, ident)
                mm.then_inc(slots_turned, 1)

            @block.vector
            def _(dve):
                did, settle = g.dve.did, g.dve.settle
                COPY, TT = nc.vector.tensor_copy, nc.vector.tensor_tensor

                def pick(src, spare, values, places, n):
                    for r in range(n // 8):
                        eight = slice(8 * r, 8 * r + 8)
                        did(nc.vector.max(values[:, eight], src))
                        settle()
                        if r < n // 8 - 1:
                            did(nc.vector.match_replace(spare, values[:, eight], src, -1.0))
                        struck_out = g.dve.mark()
                        did(nc.vector.max_index(places[:, eight], values[:, eight], src))
                        settle(struck_out)
                        src, spare = spare, src

                pick(g.aff_rows[0:E, 0:PROMPT], spare[0:E, 0:PROMPT], top_p, at_p, CAP_P)
                settle()
                did(COPY(at_pf[:], at_p[:]), picked)
                pick(g.aff_rows[:, PROMPT:], spare[:], top, at, CAP_L)
                dve.wait_ge(slots_turned, 1)
                did(COPY(prompt_slots[:], ps[1][0:CAP_P, 0:2 * E]), picked)
                settle()
                did(COPY(at_f[:], at[:]))
                did(COPY(top_b[:], top[SECOND:HALVES, ::-1]))
                settle()
                did(nc.vector.tensor_scalar(at_b[:], at_f[SECOND:HALVES, ::-1], float(PROMPT + LATENT // 2), None, ALU.add), picked)
                did(nc.vector.tensor_scalar(at_f[0:E, :], at_f[0:E, :], float(PROMPT), None, ALU.add), picked)
                dve.wait_ge(slots_turned, 3)
                did(COPY(gate_b[:], ps[0][:, 2 * E:3 * E]))
                did(COPY(row_b[:], ps[0][:, 3 * E:4 * E]))
                did(COPY(g.slot_gate_p[:], ps[1][:, 2 * E:3 * E]))
                did(nc.vector.tensor_scalar(g.slot_row_p[:], ps[1][:, 3 * E:4 * E], float(DT), g.piece[:], ALU.mult, ALU.add))
                settle()
                did(TT(first_wins[:], ps[0][:, 0:E], gate_b[:], ALU.is_ge))
                did(TT(g.slot_gate[:], ps[0][:, 0:E], gate_b[:], ALU.max))
                did(TT(gap[:], ps[0][:, E:2 * E], row_b[:], ALU.subtract))
                settle()
                did(TT(gap[:], gap[:], first_wins[:], ALU.mult))
                settle()
                did(TT(row_f[:], gap[:], row_b[:], ALU.add))
                settle()
                did(COPY(g.slot_row[:], row_f[:]))
                settle()


def experts(nc, g):
    N = CAP_L + CAP_P
    ctx = ExitStack()
    with ctx:
        def sb(name, shape):
            return ctx.enter_context(nc.sbuf_tensor(name, shape, F32))

        xe, xe_p = sb("xe", [P, D]), sb("xe_p", [P, P])
        xeT = sb("xeT", [P, DT, N])
        silu = sb("silu", [P, 2, N])
        hT = sb("hidT", [P, FT, N])
        yT, yT_p = sb("yT", [P, DT, CAP_L]), sb("yT_p", [P, DT, CAP_P])
        ye, ye_p = sb("ye", [P, D]), sb("ye_p", [P, P])
        normed_pieces, stream_pieces = (x.rearrange("r (k c) -> (r k) c", c=P) for x in (g.normed, g.stream))
        free_mark = sb("free_mark", [1, 1])
        ps_ab = [ctx.enter_context(nc.psum_tensor(f"ps_ab{i}", [P, 512], F32)) for i in range(2)]
        ps_yy = [ctx.enter_context(nc.psum_tensor(f"ps_yy{i}", [P, 512], F32)) for i in range(2)]
        ps_t = [ctx.enter_context(nc.psum_tensor(f"ps_t{i}", [P, 512], F32)) for i in range(3)]
        sem = g.sem
        h_kept, yT_kept, ye_kept, ye_free = sem("h_kept"), sem("yT_kept"), sem("ye_kept"), sem("ye_free")
        gathered, scattered, silu_ready = sem("gathered"), sem("scattered"), sem("silu_ready")
        ab_summed, y_done = g.ab_summed, g.y_done
        xe_turned, xT_act, xT_dve = sem("xe_turned"), sem("xT_act"), sem("xT_dve")
        y_turned, xp_scaled = sem("y_turned"), sem("xp_scaled")

        with nc.Block() as block:
            @block.sync
            def _(sp):
                for p in range(g.RING // 2, 8):
                    g.load_pair(sp, 0, p)
                for q in range(8):
                    g.load_w2(sp, 0, q)
                with sp.Fori(1, E) as e:
                    for p in range(8):
                        g.load_pair(sp, e, p)
                    for q in range(8):
                        g.load_w2(sp, e, q)

            @block.gpsimd
            def _(pool):
                def gather(e):
                    nc.gpsimd.indirect_dma_start(xe[:], None, g.normed, bass.IndirectOffsetOnAxis(ap=g.slot_row[:, e:e + 1], axis=0)).then_inc(gathered, 16)
                    nc.gpsimd.indirect_dma_start(xe_p[:], None, normed_pieces, bass.IndirectOffsetOnAxis(ap=g.slot_row_p[:, e:e + 1], axis=0)).then_inc(gathered, 16)

                nc.gpsimd.memset(free_mark[:], 0.0).then_inc(ye_free, 1)
                gather(0)
                for e in range(E):
                    pool.wait_ge(xe_turned, e + 1)
                    pool.wait_ge(gathered, 32 * (e + 1))
                    gather(min(e + 1, E - 1))
                    pool.wait_ge(ye_kept, 3 * (e + 1) + 1)
                    nc.gpsimd.indirect_dma_start(g.stream, bass.IndirectOffsetOnAxis(ap=g.slot_row[:, e:e + 1], axis=0), ye[:], None,
                                                 compute_op=ALU.add).then_inc(scattered, 16)
                    nc.gpsimd.indirect_dma_start(stream_pieces, bass.IndirectOffsetOnAxis(ap=g.slot_row_p[:, e:e + 1], axis=0), ye_p[:], None,
                                                 compute_op=ALU.add).then_inc(scattered, 16)
                    pool.wait_ge(scattered, 32 * (e + 1))
                    nc.gpsimd.memset(free_mark[:], 0.0).then_inc(ye_free, 1)

            @block.scalar
            def _(act):
                did = g.act.did

                def keep_x():
                    for k in range(4):
                        did(nc.scalar.activation(xeT[:, k, 0:CAP_L], ps_t[0][:, bass.ts(k, P)], ACT.Identity, scale=g.mod[:, 1, 2, k:k + 1],
                                                 bias=g.mod[:, 1, 3, k:k + 1]), xT_act if k == 3 else None)

                act.wait_ge(xe_turned, 1)
                keep_x()
                with act.Fori(0, E) as e:
                    for f in range(FT):
                        act.wait_ge(ab_summed, e * FT + (f + 1))
                        act.wait_ge(h_kept, e * FT + (f + 1))
                        nc.scalar.activation(silu[:, f % 2], ps_ab[f % 2][:, 0:N], ACT.Silu).then_inc(silu_ready, 1)
                    act.wait_ge(xe_turned, e + 2)
                    keep_x()
                    for d in range(DT):
                        act.wait_ge(y_done, e * DT + (d + 1))
                        nc.scalar.activation(yT[:, d], ps_yy[d % 2][:, 0:CAP_L], ACT.Copy, scale=g.mod[:, 1, 4, d:d + 1])
                        nc.scalar.activation(yT_p[:, d], ps_yy[d % 2][:, CAP_L:N], ACT.Copy, scale=g.mod[:, 0, 4, d:d + 1]).then_inc(yT_kept, 1)

            @block.tensor
            def _(pe):
                def turn_x():
                    for k in range(DT):
                        nc.tensor.transpose(ps_t[k // 4][:, bass.ts(k % 4, P)], xe[:, bass.ts(k, P)], g.ident)
                    nc.tensor.transpose(ps_t[2][:, 0:P], xe_p[:], g.ident).then_inc(xe_turned, 1)

                pe.wait_ge(gathered, 32)
                turn_x()
                pe.wait_ge(h_kept, 2)
                pe.wait_ge(yT_kept, 2)
                with pe.Fori(0, E) as e:
                    pe.wait_ge(xT_act, e + 1)
                    pe.wait_ge(xT_dve, e + 1)
                    for f in range(FT):
                        pe.wait_ge(h_kept, e * FT + (f + 1))
                        p, c = divmod(f, 2)
                        for w in range(2):
                            s, turn = g.slot(2 * p + w)
                            if c == 0:
                                pe.wait_ge(g.slot_loaded[s], e * 32 + 16 * (turn + 1))
                            unit = g.ring[:, s].rearrange("p (k n) -> p k n", k=DT)
                            for k in range(DT):
                                mm = nc.tensor.matmul(ps_ab[f % 2][:, N * w:N * w + N], unit[:, k, bass.ts(c, P)], xeT[:, k],
                                                      start=(k == 0), stop=(k == DT - 1))
                        mm.then_inc(ab_summed, 1)
                    pe.wait_ge(ye_kept, e * 3 + 1)
                    pe.wait_ge(gathered, e * 32 + 64)
                    turn_x()
                    pe.wait_ge(h_kept, e * FT + (FT + 2))
                    for d in range(DT):
                        pe.wait_ge(yT_kept, e * DT + (d + 1))
                        for f in range(FT):
                            s, turn = g.slot(16 + f // 2)
                            if d == 0 and f % 2 == 0:
                                pe.wait_ge(g.slot_loaded[s], e * 32 + 16 * (turn + 1))
                            unit = g.ring[:, s].rearrange("p (c n) -> p c n", c=2)
                            mm = nc.tensor.matmul(ps_yy[d % 2][:, 0:N], unit[:, f % 2, bass.ts(d, P)], hT[:, f], start=(f == 0), stop=(f == FT - 1))
                            if d == DT - 1 and f % 2 and f < FT - 1:
                                mm.then_inc(g.w2_used, 1)
                        mm.then_inc(y_done, 1)
                    pe.wait_ge(xT_act, e + 2)
                    pe.wait_ge(xT_dve, e + 2)
                    for h in range(2):
                        pe.wait_ge(yT_kept, e * DT + (DT // 2 * (h + 1) + 2))
                        for k in range(4):
                            mm = nc.tensor.transpose(ps_t[h][:, bass.ts(k, P)], yT[:, 4 * h + k], g.ident)
                        mm.then_inc(y_turned, 1)
                    nc.tensor.transpose(ps_t[2][:, 0:P], yT_p[:].rearrange("p k s -> p (k s)"), g.ident).then_inc(y_turned, 1)

            @block.vector
            def _(dve):
                did = g.dve.did
                for b in range(2):
                    did(nc.vector.memset(silu[:, b], 0.0), h_kept)
                    did(nc.vector.memset(yT[:, b], 0.0), yT_kept)
                did(nc.vector.memset(ye_p[:], 0.0), ye_kept)
                g.dve.settle()

                def keep_x(n):
                    prompt = xeT[:, :, CAP_L:N]
                    wide = [P, DT, CAP_P]
                    scale, shift = (g.mod[:, 0, v, :, None].to_broadcast(wide) for v in (2, 3))
                    nc.vector.tensor_tensor(prompt, ps_t[2][:, 0:P].rearrange("p (k s) -> p k s", s=CAP_P), scale, ALU.mult).then_inc(xp_scaled, 1)
                    for k in range(4, DT):
                        nc.vector.tensor_scalar(xeT[:, k, 0:CAP_L], ps_t[1][:, bass.ts(k - 4, P)], g.mod[:, 1, 2, k:k + 1], g.mod[:, 1, 3, k:k + 1],
                                                ALU.mult, ALU.add)
                    dve.wait_ge(xp_scaled, n)
                    nc.vector.tensor_tensor(prompt, prompt, shift, ALU.add).then_inc(xT_dve, 1)

                dve.wait_ge(xe_turned, 1)
                keep_x(1)
                with dve.Fori(0, E) as e:
                    for f in range(FT):
                        dve.wait_ge(silu_ready, e * FT + (f + 1))
                        nc.vector.tensor_tensor(hT[:, f], silu[:, f % 2], ps_ab[f % 2][:, N:2 * N], ALU.mult).then_inc(h_kept, 1)
                    dve.wait_ge(xe_turned, e + 2)
                    keep_x(e + 2)
                    for h in range(2):
                        dve.wait_ge(y_turned, e * 3 + (h + 1))
                        if h == 0:
                            dve.wait_ge(ye_free, e + 1)
                        cols = bass.ts(h, 512)
                        nc.vector.tensor_scalar(ye[:, cols], ps_t[h][:], g.slot_gate[:, bass.ds(e, 1)], None, ALU.mult).then_inc(ye_kept, 1)
                    dve.wait_ge(y_turned, e * 3 + 3)
                    nc.vector.tensor_scalar(ye_p[:], ps_t[2][:, 0:P], g.slot_gate_p[:, bass.ds(e, 1)], None, ALU.mult).then_inc(ye_kept, 1)


def finish(nc, g):
    ctx = ExitStack()
    with ctx:
        def sb(name, shape):
            return ctx.enter_context(nc.sbuf_tensor(name, shape, F32))

        xs = sb("xs", [P, TILES, D])
        final_g = sb("final_g_row", [P, D])
        squares = ctx.enter_context(nc.sbuf_tensor("squares3", [P, D], mybir.dt.bfloat16))
        ms = sb("ms3", [P, TILES])
        rs = sb("rs3", [P, TILES])
        tile_loaded, weights_end = g.slot_loaded, 32 * E
        gain_loaded, summed, inverted, scaled, outputs_stored = (
            g.sem(n) for n in ("gain_loaded", "summed", "inverted", "scaled", "outputs_stored"))

        with nc.Block() as block:
            @block.sync
            def _(sp):
                sp.dma_start(final_g[:], g.final_g.to_broadcast([P, D])).then_inc(gain_loaded, 16)
                for i in range(TILES):
                    sp.dma_start(xs[:, i], g.stream[bass.ts(i, P), :]).then_inc(tile_loaded[i], 16)
                for i in range(TILES):
                    sp.wait_ge(scaled, i + 1)
                    dst = g.y_prompt_out if i == 0 else g.y_latent_out[bass.ts(i - 1, P), :]
                    sp.dma_start(dst, xs[:, i]).then_inc(outputs_stored, 16)
                sp.wait_ge(outputs_stored, 16 * TILES)

            @block.scalar
            def _(act):
                for i in range(TILES):
                    act.wait_ge(tile_loaded[i], weights_end + 16)
                    if i:
                        g.act.settle()
                    g.act.did(nc.scalar.activation(squares[:], xs[:, i], ACT.Square, scale=D ** -0.5, accum_out=ms[:, i:i + 1]), summed)

            @block.gpsimd
            def _(pool):
                for i in range(TILES):
                    pool.wait_ge(summed, i + 1)
                    nc.gpsimd.tensor_tensor(rs[:, i:i + 1], ms[:, i:i + 1], g.eps[:], ALU.add).then_inc(inverted, 1)
                    pool.wait_ge(inverted, 2 * i + 1)
                    nc.gpsimd.tensor_tensor(rs[:, i:i + 1], rs[:, i:i + 1], g.minus_half[:, 0:1], ALU.pow).then_inc(inverted, 1)

            @block.vector
            def _(dve):
                dve.wait_ge(gain_loaded, 16)
                for i in range(TILES):
                    dve.wait_ge(inverted, 2 * i + 2)
                    dve.wait_ge(tile_loaded[i], weights_end + 16)
                    g.dve.did(nc.vector.scalar_tensor_tensor(xs[:, i], xs[:, i], rs[:, i:i + 1], final_g[:], ALU.mult, ALU.mult), scaled)


def constants():
    import numpy as np

    def dft(n):
        a = 2 * np.pi * (np.outer(np.arange(n), np.arange(n)) % n) / n
        return np.cos(a), np.sin(a)

    c64, s64 = dft(GRID_W)
    c128, s128 = dft(P)
    c16, s16 = dft(GRID_H)
    two, eight = np.eye(P // GRID_W), np.eye(8)
    pick_lane = np.zeros((P, LANES, P))
    for r in range(LANES):
        pick_lane[32 * (r // HEADS) + r % HEADS, r] = 1
    pick2 = np.zeros((P, 2, P))
    pick2[0, 0], pick2[1, 1] = 1, 1
    s, l = np.arange(P)[:, None], np.arange(P)[None, :]
    masks = np.stack([np.where(s <= l, 0, MASKED), np.where(s >= l, 0, MASKED)], 1)
    parts = {
        "ident": np.eye(P),
        "dft_cols": np.concatenate([np.kron(two, c64), -np.kron(two, s64)], 1),
        "dft_prompt": np.concatenate([c128, -s128], 1),
        "dft_chan_r": np.concatenate([c128, -s128], 1),
        "dft_chan_i": np.concatenate([s128, c128], 1),
        "dft_row_c": np.kron(c16, eight),
        "dft_row_s": np.kron(s16, eight),
        "pick_lane": pick_lane.reshape(P, -1),
        "pick2": pick2.reshape(P, -1),
        "masks": masks.reshape(P, -1),
        "spread_slots": np.concatenate([np.tile(np.eye(CAP_P), (1, DT)), np.zeros((P - CAP_P, P))], 0),
        "piece": np.arange(P)[:, None] // CAP_P,
    }
    spans, at = {}, 0
    for name, a in parts.items():
        spans[name] = (at, at + a.shape[1])
        at += a.shape[1]
    return np.concatenate(list(parts.values()), 1).astype(np.float32), spans


def weight_loads(g):
    w1, w3 = (w.rearrange("e (k p) f -> e p k f", p=P) for w in (g.exp_w1, g.exp_w3))
    w2 = g.exp_w2.rearrange("e (q c p) d -> e q p c d", c=2, p=P)

    def slot(j):
        return j % g.RING, j // g.RING

    def expert(w, e):
        return w[e] if isinstance(e, int) else w[bass.ds(e, 1)].rearrange("a p k f -> (a p) k f")

    def wait_unit(sp, e, j):
        if j < 0:
            if isinstance(e, int):
                return
            e, j = e - 1, j + 24
        if j < 16:
            sp.wait_ge(g.ab_summed, e * FT + 2 * (j // 2 + 1))
        elif j < 23:
            sp.wait_ge(g.w2_used, e * 7 + (j - 15))
        else:
            sp.wait_ge(g.y_done, e * DT + DT)

    def load_pair(sp, e, p):
        for n, w in enumerate((w1, w3)):
            s, _ = slot(2 * p + n)
            wait_unit(sp, e, 2 * p + n - g.RING)
            sp.dma_start(g.ring[:, s].rearrange("p (k n) -> p k n", k=DT), expert(w, e)[:, :, bass.ts(p, 256)]).then_inc(g.slot_loaded[s], 16)

    def load_w2(sp, e, q):
        s, _ = slot(16 + q)
        wait_unit(sp, e, 16 + q - g.RING)
        src = w2[e, q] if isinstance(e, int) else w2[bass.ds(e, 1), q].rearrange("a p c d -> (a p) c d")
        sp.dma_start(g.ring[:, s].rearrange("p (c n) -> p c n", c=2), src).then_inc(g.slot_loaded[s], 16)

    g.slot, g.load_pair, g.load_w2 = slot, load_pair, load_w2


def build(nc, t, spans):
    ctx = ExitStack()
    g = Shared()
    g.x_prompt, g.x_latent, g.state_C = t["x_prompt"], t["x_latent"], t["state_C"]
    g.state_n, g.state_m, g.c = t["state_n"], t["state_m"], t["c"]
    g.c_ctx, g.ada_w, g.ada_b = t["c_ctx"], t["ada_w"], t["ada_b"]
    g.norm1_g, g.norm2_g, g.w_in = t["norm1_g"], t["norm2_g"], t["w_in"]
    g.b_in, g.head_g, g.w_out = t["b_in"], t["head_g"], t["w_out"]
    g.router_w, g.exp_w1, g.exp_w3 = t["router_w"], t["exp_w1"], t["exp_w3"]
    g.exp_w2, g.final_g, g.constants = t["exp_w2"], t["final_g"], t["constants"]
    g.y_prompt_out, g.y_latent_out, g.new_C = t["y_prompt_out"], t["y_latent_out"], t["new_C"]
    g.new_n, g.new_m = t["new_n"], t["new_m"]
    with ctx:
        def sb(name, shape, stack=ctx, dt=F32):
            return stack.enter_context(nc.sbuf_tensor(name, shape, dt))

        def sem(name):
            return ctx.enter_context(nc.semaphore(name))

        def dram(name, shape):
            return nc.dram_tensor(name, shape, F32, kind="Internal").ap()

        g.sem = sem
        g.act = Steps(nc.scalar, sem("act_steps"))
        g.dve = Steps(nc.vector, sem("dve_steps"))
        g.kvo = dram("kvo", [ROWS, 3 * WIDTH])
        g.qkT = dram("qkT_dram", [ROWS, 2 * WIDTH])
        g.m_lanes = dram("m_lanes", [TILES, LANES * P])
        g.stream = dram("stream", [ROWS, D])
        g.normed = dram("normed", [ROWS, D])
        g.ada_b_row = g.ada_b.rearrange("a b -> (a b)")[None, :]
        g.b_in_col = g.b_in.rearrange("a b -> (a b)")[:, None]
        g.w_in_src = g.w_in.rearrange("(k p) n -> p k n", p=P)
        g.w_out_src = g.w_out.rearrange("(k p) n -> p k n", p=P)
        g.x_rows = lambda i: g.x_prompt if isinstance(i, int) and i == 0 else g.x_latent[bass.ts(i - 1, P), :]

        g.const = sb("const", [P, max(b for _, b in spans.values())])
        part = {name: g.const[:, a:b] for name, (a, b) in spans.items()}
        g.ident, g.dft_cols, g.dft_prompt, g.dft_chan_r, g.dft_chan_i = (
            part["ident"], part["dft_cols"], part["dft_prompt"], part["dft_chan_r"], part["dft_chan_i"])
        g.dft_row_c, g.dft_row_s, g.pick_lane, g.pick2, g.masks = (
            part["dft_row_c"], part["dft_row_s"], part["pick_lane"], part["pick2"], part["masks"])
        g.spread_slots, g.piece = part["spread_slots"], part["piece"]
        g.mod = sb("mod", [P, 2, 5, DT])
        g.gate1 = sb("gate1", [P, 2, D])
        g.minus_half = sb("minus_half", [P, HEADS])
        g.eps = sb("eps", [P, 1])
        g.aff_rows = sb("aff_rows", [HALVES, PROMPT + LATENT // 2])
        g.w_in_loaded = sem("w_in_loaded")
        g.b_in_loaded = sem("b_in_loaded")
        g.w_out_loaded = sem("w_out_loaded")
        with ExitStack() as mixer:
            g.cols = sb("cols", [P, 4, TILES, LANES], mixer)
            shared = sb("m_rows", [P, ROWS], mixer)
            g.m_row = shared[0:64, :]
            g.w_gate = shared[:, 0:D].rearrange("p (k n) -> p k n", k=DT)
            with ExitStack() as heads:
                g.y = sb("y", [P, 4, 2, LATENT], heads)[:]
                g.y_prompt = sb("y_prompt", [P, 4, 2, PROMPT], heads)
                g.gate_rows = sb("gate_rows", [P, ROWS], heads)
                with ExitStack() as weights:
                    g.w_in_sb = sb("w_in_sb", [P, DT, IN_COLS], weights)
                    g.b_in_row = sb("b_in_row", [P, IN_COLS], weights)
                    g.xt, g.xn, g.ms = sb("xt", [P, 2, D], weights), sb("xn", [P, D], weights), sb("ms", [P, 2, 4], weights)
                    g.squares = sb("squares", [P, D], weights, mybir.dt.bfloat16)
                    g.x_loaded = [sem(f"x_loaded{i}") for i in range(2)]
                    g.squares_summed, g.rms_inverted = sem("squares_summed"), sem("rms_inverted")
                    g.x_normed, g.x_turned = sem("x_normed"), sem("x_turned")
                    modulation(nc, g)
                    projection(nc, g)
                g.states = sb("states", [P, TILES, LANES, VW], heads)
                g.fuT = sb("fuT", [P, 4, ROWS], heads)
                g.end_states, g.end_n = sb("end_states", [P, LANES, HD], heads), sb("end_n", [LANES, HD], heads)
                g.states_stored = sem("states_stored")
                recurrence(nc, g)
                g.w_out_sb = g.y.rearrange("p a b n -> p (a b n)").rearrange("p (k n) -> p k n", k=DT)
                mixing(nc, g)
        g.slot_gate, g.slot_gate_p = sb("slot_gate", [P, E]), sb("slot_gate_p", [P, E])
        g.slot_row, g.slot_row_p = sb("slot_row", [P, E], dt=U32), sb("slot_row_p", [P, E], dt=U32)
        g.RING = 12
        with ExitStack() as weights:
            g.ring = sb("ring", [P, g.RING, 2 * D], weights)
            g.slot_loaded = [sem(f"slot_loaded{i}") for i in range(g.RING)]
            g.ab_summed, g.w2_used, g.y_done = sem("ab_summed"), sem("w2_used"), sem("y_done")
            weight_loads(g)
            routing(nc, g)
            experts(nc, g)
        finish(nc, g)


_INPUTS = {
    "x_prompt": ("x_prompt", (PROMPT, D)), "x_latent": ("x_sample", (LATENT, D)),
    "state_C": ("state_C", (LANES * HD, HD)), "state_n": ("state_n", (LANES, HD)), "state_m": ("state_m", (LANES, 1)),
    "c": ("c", (DT, P)), "c_ctx": ("c_ctx", (DT, P)), "ada_w": ("ada_w", (D, MOD_COLS)), "ada_b": ("ada_b", (MOD_T, P)),
    "norm1_g": ("norm1_g", (DT, P)), "norm2_g": ("norm2_g", (DT, P)), "w_in": ("w_in", (D, IN_COLS)), "b_in": ("b_in", (1, IN_COLS)),
    "head_g": ("head_g", (1, WIDTH)), "w_out": ("w_out", (D, D)), "router_w": ("router_w", (D, E)),
    "exp_w1": ("exp_w1", (E, D, F)), "exp_w3": ("exp_w3", (E, D, F)), "exp_w2": ("exp_w2", (E, F, D)), "final_g": ("final_g", (1, D)),
}
_OUTPUTS = {
    "y_prompt_out": (PROMPT, D), "y_latent_out": (LATENT, D),
    "new_C": (LANES * HD, HD), "new_n": (LANES, HD), "new_m": (LANES, 1),
}


def kernel(**inputs):
    import numpy as np
    import concourse.bacc as bacc
    from concourse.bass_utils import run_bass_kernel_spmd

    nc = bacc.Bacc("TRN2", target_bir_lowering=False, num_devices=1)
    table, spans = constants()
    arrays = {name: np.ascontiguousarray(np.asarray(inputs[key]).reshape(shape)) for name, (key, shape) in _INPUTS.items()}
    arrays["constants"] = table
    t = {name: nc.dram_tensor(f"in_{name}", a.shape, mybir.dt.from_np(a.dtype), kind="ExternalInput").ap()
         for name, a in arrays.items()}
    for name, shape in _OUTPUTS.items():
        t[name] = nc.dram_tensor(f"out_{name}", shape, F32, kind="ExternalOutput").ap()
    build(nc, t, spans)
    r = run_bass_kernel_spmd(nc, [{f"in_{name}": a for name, a in arrays.items()}], core_ids=[0]).results[0]
    return (
        r["out_y_prompt_out"].reshape(1, PROMPT, D),
        r["out_y_latent_out"].reshape(1, LATENT, D),
        r["out_new_C"].reshape(1, 1, 2, HEADS, HD, HD),
        r["out_new_n"].reshape(1, 1, 2, HEADS, HD),
        r["out_new_m"].reshape(1, 1, 2, HEADS),
    )
```
